# Optimizing a Trainium2 kernel written in Bass

```python
import math
import jax, jax.numpy as jnp
from jax import lax
import numpy as np

D_MODEL = 1024
BATCH = 1
SEQ = 256
DEPTH = 2

PLE_DIM = 256
NSA_HEADS = 8
NSA_HEAD_DIM = 64
NSA_GROUPS = 2
NSA_Q_PER_GROUP = NSA_HEADS // NSA_GROUPS
CMP_BLOCK = 32
CMP_STRIDE = 16
CMP_HIDDEN = 4 * NSA_HEAD_DIM
SLC_BLOCK = 64
N_SELECT = 16
WINDOW = 512
Q_BLOCK = 128
RET_HEADS = 4
RET_HEAD_DIM = 128
RET_CHUNK = 128
ROPE_BASE = 10000.0
D_FF = 4 * D_MODEL
EPS = 1e-6
MASK_VALUE = -1e30
FORCE_SCORE = 1e4

NSA_Q_W = NSA_HEADS * NSA_HEAD_DIM
NSA_KV_W = NSA_GROUPS * NSA_HEAD_DIM
NSA_GATE_W = 3 * NSA_HEADS
RET_W = RET_HEADS * RET_HEAD_DIM
IN_SPLITS = (NSA_Q_W, NSA_KV_W, NSA_KV_W, NSA_KV_W, NSA_KV_W, NSA_KV_W, NSA_KV_W, NSA_GATE_W,
             RET_W, RET_W, RET_W, RET_W, D_MODEL, D_MODEL)
D_IN = sum(IN_SPLITS)


def split_cols(z, sizes):
    out = []
    off = 0
    for s in sizes:
        out.append(z[..., off:off + s])
        off += s
    return out

def rmsnorm(x, g):
    xf = x.astype(jnp.float32)
    y = xf * lax.rsqrt(jnp.mean(xf * xf, axis=-1, keepdims=True) + EPS)
    return (y * g.astype(jnp.float32)).astype(x.dtype)

def rms_noaffine(x):
    xf = x.astype(jnp.float32)
    return xf * lax.rsqrt(jnp.mean(xf * xf, axis=-1, keepdims=True) + EPS)

def masked_softmax(s, mask):
    s = jnp.where(mask, s, MASK_VALUE)
    m = jnp.max(s, axis=-1, keepdims=True)
    e = jnp.exp(s - m) * mask
    return e / jnp.maximum(jnp.sum(e, axis=-1, keepdims=True), 1e-30)

def rope(x, pos):
    half = x.shape[-1] // 2
    inv = ROPE_BASE ** (-jnp.arange(half, dtype=jnp.float32) / half)
    ang = pos[:, None] * inv[None, :]
    cos = jnp.cos(ang)[:, None, :]
    sin = jnp.sin(ang)[:, None, :]
    x1 = x[..., :half].astype(jnp.float32)
    x2 = x[..., half:].astype(jnp.float32)
    return jnp.concatenate([x1 * cos - x2 * sin, x1 * sin + x2 * cos], axis=-1)

def nsa_mixer(q_in, kc_in, vc_in, ks_in, vs_in, kw_in, vw_in, gate_logits,
              qn_g, kn_g, pos_k, pos_v, w1_k, w2_k, w1_v, w2_v):
    B, S = q_in.shape[:2]
    G, Hg, dh = NSA_GROUPS, NSA_Q_PER_GROUP, NSA_HEAD_DIM
    dtype = q_in.dtype
    scale = dh ** -0.5
    q = rmsnorm(q_in.reshape(B, S, G, Hg, dh).transpose(0, 2, 3, 1, 4), qn_g)

    def kv_heads(z):
        return z.reshape(B, S, G, dh).transpose(0, 2, 1, 3)

    k_c, v_c = kv_heads(kc_in), kv_heads(vc_in)
    k_s, v_s = rmsnorm(kv_heads(ks_in), kn_g), kv_heads(vs_in)
    k_w, v_w = rmsnorm(kv_heads(kw_in), kn_g), kv_heads(vw_in)
    gates = jax.nn.sigmoid(gate_logits.astype(jnp.float32)).reshape(B, S, 3, G, Hg).transpose(0, 3, 4, 1, 2)

    nc = S // CMP_STRIDE
    starts = jnp.arange(nc) * CMP_STRIDE
    idx = jnp.minimum(starts[:, None] + jnp.arange(CMP_BLOCK)[None, :], S - 1)
    cmp_end = starts + CMP_BLOCK - 1

    def compress(z, pos, w1, w2):
        zb = (z[:, :, idx] + pos).reshape(B, G, nc, CMP_BLOCK * dh)
        return jax.nn.gelu(zb @ w1) @ w2

    k_cmp = rmsnorm(compress(k_c, pos_k, w1_k, w2_k), kn_g)
    v_cmp = compress(v_c, pos_v, w1_v, w2_v)

    ns = S // SLC_BLOCK
    n_sel = min(N_SELECT, ns)
    ratio = SLC_BLOCK // CMP_STRIDE
    k_blk = k_s.reshape(B, G, ns, SLC_BLOCK, dh)
    v_blk = v_s.reshape(B, G, ns, SLC_BLOCK, dh)
    b_ix = jnp.arange(B)[:, None, None, None]
    g_ix = jnp.arange(G)[None, :, None, None]

    pad = ((0, 0), (0, 0), (WINDOW, 0), (0, 0))
    k_w_pad = jnp.pad(k_w, pad)
    v_w_pad = jnp.pad(v_w, pad)

    def query_block(c):
        q0 = c * Q_BLOCK
        qc = lax.dynamic_slice_in_dim(q, q0, Q_BLOCK, axis=3)
        gc = lax.dynamic_slice_in_dim(gates, q0, Q_BLOCK, axis=3)
        t = q0 + jnp.arange(Q_BLOCK)

        s = jnp.einsum('bghqd,bgnd->bghqn', qc, k_cmp).astype(jnp.float32) * scale
        p_cmp = masked_softmax(s, cmp_end[None, :] <= t[:, None])
        o_cmp = jnp.einsum('bghqn,bgnd->bghqd', p_cmp.astype(dtype), v_cmp)

        imp = jnp.sum(p_cmp, axis=2).reshape(B, G, Q_BLOCK, ns, ratio)
        imp_blk = jnp.sum(imp, axis=-1) + jnp.pad(imp[..., :-1, -1], ((0, 0), (0, 0), (0, 0), (1, 0)))
        blk = jnp.arange(ns)[None, :]
        cur = (t // SLC_BLOCK)[:, None]
        forced = (blk == 0) | (blk == cur) | (blk == cur - 1)
        score = jnp.where(forced, FORCE_SCORE, imp_blk)
        score = jnp.where(blk > cur, MASK_VALUE, score)
        _, sel = lax.top_k(score, n_sel)
        ks = k_blk[b_ix, g_ix, sel]
        vs = v_blk[b_ix, g_ix, sel]
        kpos = sel[..., None] * SLC_BLOCK + jnp.arange(SLC_BLOCK)
        smask = (kpos <= t[:, None, None]).reshape(B, G, Q_BLOCK, n_sel * SLC_BLOCK)[:, :, None]
        s = jnp.einsum('bghqd,bgqnkd->bghqnk', qc, ks).astype(jnp.float32) * scale
        p_slc = masked_softmax(s.reshape(B, G, Hg, Q_BLOCK, n_sel * SLC_BLOCK), smask)
        o_slc = jnp.einsum('bghqnk,bgqnkd->bghqd',
                           p_slc.reshape(B, G, Hg, Q_BLOCK, n_sel, SLC_BLOCK).astype(dtype), vs)

        kw = lax.dynamic_slice_in_dim(k_w_pad, q0, Q_BLOCK + WINDOW, axis=2)
        vw = lax.dynamic_slice_in_dim(v_w_pad, q0, Q_BLOCK + WINDOW, axis=2)
        wpos = q0 - WINDOW + jnp.arange(Q_BLOCK + WINDOW)
        dist = t[:, None] - wpos[None, :]
        wmask = (dist >= 0) & (dist < WINDOW) & (wpos[None, :] >= 0)
        s = jnp.einsum('bghqd,bgkd->bghqk', qc, kw).astype(jnp.float32) * scale
        p_win = masked_softmax(s, wmask)
        o_win = jnp.einsum('bghqk,bgkd->bghqd', p_win.astype(dtype), vw)

        return gc[..., 0:1] * o_cmp + gc[..., 1:2] * o_slc + gc[..., 2:3] * o_win

    out = lax.map(query_block, jnp.arange(S // Q_BLOCK))
    return out.transpose(1, 0, 4, 2, 3, 5).reshape(B, S, NSA_Q_W).astype(dtype)

def retention(q_in, k_in, v_in, g_in):
    B, S = q_in.shape[:2]
    H, dk, C = RET_HEADS, RET_HEAD_DIM, RET_CHUNK
    dtype = q_in.dtype
    pos = jnp.arange(S, dtype=jnp.float32)
    q = rope(q_in.reshape(B, S, H, dk), pos)
    k = rope(k_in.reshape(B, S, H, dk), pos) * (dk ** -0.5)
    v = v_in.reshape(B, S, H, dk).astype(jnp.float32)
    nch = S // C

    def chunks(z):
        return z.reshape(B, nch, C, H, dk).transpose(0, 3, 1, 2, 4)

    qc, kc, vc = chunks(q), chunks(k), chunks(v)
    gamma = 1.0 - 2.0 ** (-5.0 - jnp.arange(H, dtype=jnp.float32))
    lg = jnp.log(gamma)
    n = jnp.arange(C, dtype=jnp.float32)
    diff = n[:, None] - n[None, :]
    decay = jnp.where(diff >= 0, jnp.exp(lg[:, None, None] * jnp.maximum(diff, 0.0)), 0.0)
    xi = jnp.exp(lg[:, None] * (n + 1.0))[None, :, None, :, None]
    zeta = jnp.exp(lg[:, None] * (C - 1.0 - n))[None, :, None, :, None]
    g_chunk = jnp.exp(lg * C)[None, :, None, None]

    inner = jnp.einsum('bhcnd,bhcmd->bhcnm', qc, kc) * decay[None, :, None]
    inner = jnp.einsum('bhcnm,bhcme->bhcne', inner, vc)
    kv = jnp.einsum('bhcmd,bhcme->cbhde', kc * zeta, vc)

    def step(R, kv_c):
        return g_chunk * R + kv_c, R

    _, R_prev = lax.scan(step, jnp.zeros((B, H, dk, dk), jnp.float32), kv)
    cross = jnp.einsum('bhcnd,cbhde->bhcne', qc * xi, R_prev)
    y = rms_noaffine(inner + cross)
    y = y.transpose(0, 2, 3, 1, 4).reshape(B, S, RET_W)
    return (jax.nn.silu(g_in.astype(jnp.float32)) * y).astype(dtype)

def first_inputs(seed: int = 0) -> dict:
    key = jax.random.key(seed)
    ks = jax.random.split(key, 21)
    f32 = jnp.float32

    def nrm(k, shape, scale):
        return jax.random.normal(k, shape, f32) * scale

    def gain(k, shape):
        return 1.0 + 0.1 * jax.random.normal(k, shape, f32)

    dh = NSA_HEAD_DIM
    return {
        "x": nrm(ks[0], (BATCH, SEQ, D_MODEL), 1.0),
        "p": nrm(ks[1], (DEPTH, BATCH, SEQ, PLE_DIM), 1.0),
        "norm_mix": gain(ks[2], (DEPTH, D_MODEL)),
        "w_in": nrm(ks[3], (DEPTH, D_MODEL, D_IN), D_MODEL ** -0.5),
        "nsa_q_norm": gain(ks[4], (DEPTH, dh)),
        "nsa_k_norm": gain(ks[5], (DEPTH, dh)),
        "cmp_pos_k": nrm(ks[6], (DEPTH, CMP_BLOCK, dh), 0.1),
        "cmp_pos_v": nrm(ks[7], (DEPTH, CMP_BLOCK, dh), 0.1),
        "cmp_w1_k": nrm(ks[8], (DEPTH, CMP_BLOCK * dh, CMP_HIDDEN), (CMP_BLOCK * dh) ** -0.5),
        "cmp_w2_k": nrm(ks[9], (DEPTH, CMP_HIDDEN, dh), CMP_HIDDEN ** -0.5),
        "cmp_w1_v": nrm(ks[10], (DEPTH, CMP_BLOCK * dh, CMP_HIDDEN), (CMP_BLOCK * dh) ** -0.5),
        "cmp_w2_v": nrm(ks[11], (DEPTH, CMP_HIDDEN, dh), CMP_HIDDEN ** -0.5),
        "w_up_nsa": nrm(ks[12], (DEPTH, NSA_Q_W, D_MODEL), NSA_Q_W ** -0.5),
        "w_up_ret": nrm(ks[13], (DEPTH, RET_W, D_MODEL), RET_W ** -0.5),
        "w_out": nrm(ks[14], (DEPTH, D_MODEL, D_MODEL), D_MODEL ** -0.5),
        "norm_mlp": gain(ks[15], (DEPTH, D_MODEL)),
        "w_ff1": nrm(ks[16], (DEPTH, D_MODEL, D_FF), D_MODEL ** -0.5),
        "w_ff2": nrm(ks[17], (DEPTH, D_FF, D_MODEL), D_FF ** -0.5),
        "norm_ple": gain(ks[18], (DEPTH, D_MODEL)),
        "w_ple": nrm(ks[19], (DEPTH, PLE_DIM, D_MODEL), PLE_DIM ** -0.5),
        "w_ple_gate": nrm(ks[20], (DEPTH, D_MODEL, D_MODEL), D_MODEL ** -0.5),
    }

def first_block(x, p, norm_mix, w_in, nsa_q_norm, nsa_k_norm, cmp_pos_k, cmp_pos_v,
              cmp_w1_k, cmp_w2_k, cmp_w1_v, cmp_w2_v, w_up_nsa, w_up_ret, w_out,
              norm_mlp, w_ff1, w_ff2, norm_ple, w_ple, w_ple_gate):
    for i in range(DEPTH):
        h = rmsnorm(x, norm_mix[i])
        z = h @ w_in[i]
        (q_a, kc, vc, ks_, vs_, kw, vw, g_nsa, rq, rk, rv, rg, merge_a, merge_b) = split_cols(z, IN_SPLITS)
        y_a = nsa_mixer(q_a, kc, vc, ks_, vs_, kw, vw, g_nsa, nsa_q_norm[i], nsa_k_norm[i],
                        cmp_pos_k[i], cmp_pos_v[i], cmp_w1_k[i], cmp_w2_k[i], cmp_w1_v[i], cmp_w2_v[i]) @ w_up_nsa[i]
        y_b = retention(rq, rk, rv, rg) @ w_up_ret[i]
        mix = jax.nn.sigmoid(merge_a) * y_a + jax.nn.sigmoid(merge_b) * y_b
        x = x + mix @ w_out[i]
        h = rmsnorm(x, norm_mlp[i])
        x = x + jnp.square(jax.nn.relu(h @ w_ff1[i])) @ w_ff2[i]
        gate = jax.nn.sigmoid(rmsnorm(x, norm_ple[i]) @ w_ple_gate[i])
        x = x + gate * (p[i] @ w_ple[i])
    return x


N_META = 16
BLOCK = 128
PAD = BLOCK - N_META
ROPE_THETA = 10000.0
NORM_EPS = 1e-6
MASK_VALUE_2 = -1e30

MLA_HEADS = 8
MLA_Q_LORA = 256
MLA_KV_LORA = 128
MLA_NOPE = 64
MLA_ROPE = 32
MLA_V = 64
MLA_QK = MLA_NOPE + MLA_ROPE
SB_HEADS = 8
SB_HEAD_DIM = 64
DIFF_HEADS = 4
DIFF_HEAD_DIM = 64
DIFF_V_DIM = 2 * DIFF_HEAD_DIM
N_BRANCHES = 3
MLA_OUT = MLA_HEADS * MLA_V
SB_OUT = SB_HEADS * SB_HEAD_DIM
DIFF_QK = DIFF_HEADS * 2 * DIFF_HEAD_DIM
DIFF_OUT = DIFF_HEADS * DIFF_V_DIM
BRANCH_WIDTH = MLA_OUT + SB_OUT + DIFF_OUT
D_FF_2 = 4 * D_MODEL
IN_SIZES = (MLA_Q_LORA, MLA_KV_LORA, MLA_ROPE,
            SB_OUT, SB_OUT, SB_OUT,
            DIFF_QK, DIFF_QK, DIFF_OUT,
            N_BRANCHES * D_MODEL)
IN_COLS = sum(IN_SIZES)


def _split_cols(t, sizes):
    outs, off = [], 0
    for s in sizes:
        outs.append(t[..., off:off + s])
        off += s
    return outs

def _rmsnorm(x, g):
    x32 = x.astype(jnp.float32)
    y = x32 * lax.rsqrt(jnp.mean(x32 * x32, axis=-1, keepdims=True) + NORM_EPS)
    return (y * g.astype(jnp.float32)).astype(x.dtype)

def _rope(x, pos):
    d = x.shape[-1]
    half = d // 2
    inv_freq = jnp.exp(-math.log(ROPE_THETA) * (2.0 * jnp.arange(half, dtype=jnp.float32) / d))
    ang = pos.astype(jnp.float32)[:, None] * inv_freq[None, :]
    cos = jnp.cos(ang).astype(x.dtype)
    sin = jnp.sin(ang).astype(x.dtype)
    x1, x2 = x[..., :half], x[..., half:]
    return jnp.concatenate([x1 * cos - x2 * sin, x1 * sin + x2 * cos], axis=-1)

def _heads(t, n_heads):
    b, p, _ = t.shape
    return t.reshape(b, p, n_heads, -1).transpose(0, 2, 1, 3)

def _to_blocks(t):
    b, h, p, d = t.shape
    return t.reshape(b, h, p // BLOCK, BLOCK, d).transpose(2, 0, 1, 3, 4)

def _from_blocks(o):
    nb, b, h, blk, d = o.shape
    return o.transpose(1, 0, 3, 2, 4).reshape(b, nb * blk, h * d)

def _scores(qb, k, scale):
    return jnp.einsum('bhqd,bhkd->bhqk', qb, k).astype(jnp.float32) * scale

def _masked_softmax(s, mask):
    return jax.nn.softmax(jnp.where(mask[None, None], s, MASK_VALUE_2), axis=-1)

def _softmax_attention(q, k, v, scale):
    p_len = q.shape[2]
    kidx = jnp.arange(p_len)
    kvalid = kidx >= PAD

    def block(args):
        qb, qi = args
        mask = (kidx[None, :] <= qi[:, None]) & kvalid[None, :]
        p = _masked_softmax(_scores(qb, k, scale), mask)
        return jnp.einsum('bhqk,bhkd->bhqd', p.astype(v.dtype), v)

    return _from_blocks(lax.map(block, (_to_blocks(q), kidx.reshape(-1, BLOCK))))

def _stick_breaking_attention(q, k, v):
    p_len = q.shape[2]
    scale = q.shape[-1] ** -0.5
    kidx = jnp.arange(p_len)
    kvalid = kidx >= PAD

    def block(args):
        qb, qi = args
        z = _scores(qb, k, scale)
        mask = ((kidx[None, :] < qi[:, None]) & kvalid[None, :])[None, None]
        log_keep = jnp.where(mask, jax.nn.log_sigmoid(-z), 0.0)
        suffix = lax.cumsum(log_keep, axis=3, reverse=True) - log_keep
        a = jnp.where(mask, jnp.exp(jax.nn.log_sigmoid(z) + suffix), 0.0)
        return jnp.einsum('bhqk,bhkd->bhqd', a.astype(v.dtype), v)

    return _from_blocks(lax.map(block, (_to_blocks(q), kidx.reshape(-1, BLOCK))))

def _differential_attention(q1, q2, k1, k2, v, lam):
    p_len = q1.shape[2]
    scale = q1.shape[-1] ** -0.5
    kidx = jnp.arange(p_len)
    kvalid = kidx >= PAD

    def block(args):
        q1b, q2b, qi = args
        mask = (kidx[None, :] <= qi[:, None]) & kvalid[None, :]
        p1 = _masked_softmax(_scores(q1b, k1, scale), mask)
        p2 = _masked_softmax(_scores(q2b, k2, scale), mask)
        w = p1 - lam * p2
        return jnp.einsum('bhqk,bhkd->bhqd', w.astype(v.dtype), v)

    return _from_blocks(lax.map(block, (_to_blocks(q1), _to_blocks(q2), kidx.reshape(-1, BLOCK))))

def second_inputs(seed: int = 0) -> dict:
    key = jax.random.key(seed)
    ks = jax.random.split(key, 24)
    f32 = jnp.float32

    def nrm(k, shape, scale):
        return jax.random.normal(k, shape, f32) * scale

    def gain(k, shape):
        return 1.0 + 0.02 * jax.random.normal(k, shape, f32)

    return {
        "x": jax.random.normal(ks[0], (BATCH, SEQ, D_MODEL), f32),
        "meta_tokens": nrm(ks[1], (N_META, D_MODEL), 1.0),
        "ln1_g": gain(ks[2], (DEPTH, D_MODEL)),
        "w_in": nrm(ks[3], (DEPTH, D_MODEL, IN_COLS), D_MODEL ** -0.5),
        "mla_cq_norm_g": gain(ks[4], (DEPTH, MLA_Q_LORA)),
        "mla_ckv_norm_g": gain(ks[5], (DEPTH, MLA_KV_LORA)),
        "mla_w_uq": nrm(ks[6], (DEPTH, MLA_Q_LORA, MLA_HEADS * MLA_QK), MLA_Q_LORA ** -0.5),
        "mla_w_ukv": nrm(ks[7], (DEPTH, MLA_KV_LORA, MLA_HEADS * (MLA_NOPE + MLA_V)), MLA_KV_LORA ** -0.5),
        "mla_q_norm_g": gain(ks[8], (DEPTH, MLA_QK)),
        "mla_k_norm_g": gain(ks[9], (DEPTH, MLA_QK)),
        "diff_q_norm_g": gain(ks[10], (DEPTH, DIFF_HEAD_DIM)),
        "diff_k_norm_g": gain(ks[11], (DEPTH, DIFF_HEAD_DIM)),
        "diff_lambda": nrm(ks[12], (DEPTH, 4, DIFF_HEAD_DIM), 0.1),
        "diff_out_norm_g": gain(ks[13], (DEPTH, DIFF_V_DIM)),
        "gate_b": nrm(ks[14], (DEPTH, N_BRANCHES * D_MODEL), 0.02),
        "w_branch": nrm(ks[15], (DEPTH, BRANCH_WIDTH, D_MODEL), MLA_OUT ** -0.5),
        "w_out": nrm(ks[16], (DEPTH, D_MODEL, D_MODEL), D_MODEL ** -0.5),
        "ln2_g": gain(ks[17], (DEPTH, D_MODEL)),
        "w_ff1": nrm(ks[18], (DEPTH, D_MODEL, D_FF_2), D_MODEL ** -0.5),
        "w_ff2": nrm(ks[19], (DEPTH, D_FF_2, D_MODEL), D_FF_2 ** -0.5),
    }

def second_block(x, meta_tokens, ln1_g, w_in, mla_cq_norm_g, mla_ckv_norm_g, mla_w_uq, mla_w_ukv,
              mla_q_norm_g, mla_k_norm_g, diff_q_norm_g, diff_k_norm_g, diff_lambda,
              diff_out_norm_g, gate_b, w_branch, w_out, ln2_g, w_ff1, w_ff2):
    b, seq, d = x.shape
    pad = jnp.zeros((b, PAD, d), x.dtype)
    meta = jnp.broadcast_to(meta_tokens.astype(x.dtype)[None], (b, N_META, d))
    h_res = jnp.concatenate([pad, meta, x], axis=1)
    p_len = h_res.shape[1]
    pos = jnp.maximum(jnp.arange(p_len) - PAD, 0)

    for layer in range(DEPTH):
        h = _rmsnorm(h_res, ln1_g[layer])
        proj = h @ w_in[layer]
        (c_q, c_kv, k_rope, sb_q, sb_k, sb_v,
         df_q, df_k, df_v, gate_logits) = _split_cols(proj, IN_SIZES)

        q = _heads(_rmsnorm(c_q, mla_cq_norm_g[layer]) @ mla_w_uq[layer], MLA_HEADS)
        kv = _heads(_rmsnorm(c_kv, mla_ckv_norm_g[layer]) @ mla_w_ukv[layer], MLA_HEADS)
        k_nope, v_mla = kv[..., :MLA_NOPE], kv[..., MLA_NOPE:]
        k_r = jnp.broadcast_to(k_rope[:, None], (b, MLA_HEADS, p_len, MLA_ROPE))
        k = jnp.concatenate([k_nope, k_r], axis=-1)
        q = _rmsnorm(q, mla_q_norm_g[layer])
        k = _rmsnorm(k, mla_k_norm_g[layer])
        q = jnp.concatenate([q[..., :MLA_NOPE], _rope(q[..., MLA_NOPE:], pos)], axis=-1)
        k = jnp.concatenate([k[..., :MLA_NOPE], _rope(k[..., MLA_NOPE:], pos)], axis=-1)
        out_a = _softmax_attention(q, k, v_mla, MLA_QK ** -0.5)

        out_b = _stick_breaking_attention(_heads(sb_q, SB_HEADS), _heads(sb_k, SB_HEADS),
                                          _heads(sb_v, SB_HEADS))

        dq = _heads(df_q, DIFF_HEADS)
        dk = _heads(df_k, DIFF_HEADS)
        dv = _heads(df_v, DIFF_HEADS)
        qn, kn = diff_q_norm_g[layer], diff_k_norm_g[layer]
        q1 = _rope(_rmsnorm(dq[..., :DIFF_HEAD_DIM], qn), pos)
        q2 = _rope(_rmsnorm(dq[..., DIFF_HEAD_DIM:], qn), pos)
        k1 = _rope(_rmsnorm(dk[..., :DIFF_HEAD_DIM], kn), pos)
        k2 = _rope(_rmsnorm(dk[..., DIFF_HEAD_DIM:], kn), pos)
        lam_init = 0.8 - 0.6 * math.exp(-0.3 * layer)
        lp = diff_lambda[layer].astype(jnp.float32)
        lam = jnp.exp(jnp.sum(lp[0] * lp[1])) - jnp.exp(jnp.sum(lp[2] * lp[3])) + lam_init
        o_c = _differential_attention(q1, q2, k1, k2, dv, lam)
        o_c = _rmsnorm(o_c.reshape(b, p_len, DIFF_HEADS, DIFF_V_DIM), diff_out_norm_g[layer])
        out_c = (o_c * (1.0 - lam_init)).reshape(b, p_len, DIFF_OUT)

        gates = jax.nn.sigmoid(gate_logits + gate_b[layer]).reshape(b, p_len, N_BRANCHES, d)
        wb_a, wb_b, wb_c = _split_cols(w_branch[layer].T, (MLA_OUT, SB_OUT, DIFF_OUT))
        merged = (gates[:, :, 0] * (out_a @ wb_a.T)
                  + gates[:, :, 1] * (out_b @ wb_b.T)
                  + gates[:, :, 2] * (out_c @ wb_c.T))
        h_res = h_res + merged @ w_out[layer]

        h2 = _rmsnorm(h_res, ln2_g[layer])
        h_res = h_res + jnp.square(jax.nn.relu(h2 @ w_ff1[layer])) @ w_ff2[layer]

    return h_res[:, PAD + N_META:]


def setup_inputs(seed=0):
    out = dict(first_inputs(seed))
    for name, value in second_inputs(seed + 1).items():
        if name != "x":
            out[name + "_2"] = value
    return out


def reference(
    x, p, norm_mix, w_in, nsa_q_norm, nsa_k_norm, cmp_pos_k, cmp_pos_v, cmp_w1_k, cmp_w2_k,
    cmp_w1_v, cmp_w2_v, w_up_nsa, w_up_ret, w_out, norm_mlp, w_ff1, w_ff2, norm_ple, w_ple,
    w_ple_gate, meta_tokens_2, ln1_g_2, w_in_2, mla_cq_norm_g_2, mla_ckv_norm_g_2, mla_w_uq_2,
    mla_w_ukv_2, mla_q_norm_g_2, mla_k_norm_g_2, diff_q_norm_g_2, diff_k_norm_g_2,
    diff_lambda_2, diff_out_norm_g_2, gate_b_2, w_branch_2, w_out_2, ln2_g_2, w_ff1_2, w_ff2_2,
):
    x = first_block(
        x, p, norm_mix, w_in, nsa_q_norm, nsa_k_norm, cmp_pos_k, cmp_pos_v, cmp_w1_k, cmp_w2_k,
        cmp_w1_v, cmp_w2_v, w_up_nsa, w_up_ret, w_out, norm_mlp, w_ff1, w_ff2, norm_ple, w_ple,
        w_ple_gate,
    )
    return second_block(
        x, meta_tokens_2, ln1_g_2, w_in_2, mla_cq_norm_g_2, mla_ckv_norm_g_2, mla_w_uq_2,
        mla_w_ukv_2, mla_q_norm_g_2, mla_k_norm_g_2, diff_q_norm_g_2, diff_k_norm_g_2,
        diff_lambda_2, diff_out_norm_g_2, gate_b_2, w_branch_2, w_out_2, ln2_g_2, w_ff1_2,
        w_ff2_2,
    )


_drawn_inputs = setup_inputs


def setup_inputs(seed=0):
    import zlib

    import numpy as np

    out = dict(_drawn_inputs(seed))
    spreads = {}
    factors = {'nsa_q_norm': 4.635,
     'nsa_k_norm': 4.069,
     'cmp_pos_k': 8.0,
     'cmp_pos_v': 3.13,
     'norm_ple': 3.335,
     'ln1_g_2': 6.541,
     'mla_cq_norm_g_2': 8.0,
     'mla_ckv_norm_g_2': 8.0,
     'mla_q_norm_g_2': 8.0,
     'mla_k_norm_g_2': 8.0,
     'diff_q_norm_g_2': 8.0,
     'diff_k_norm_g_2': 8.0,
     'diff_lambda_2': 8.0,
     'diff_out_norm_g_2': 8.0,
     'gate_b_2': 8.0,
     'ln2_g_2': 3.762}
    for name, (base, spread) in spreads.items():
        noise = np.random.default_rng([zlib.crc32(name.encode()), seed]).standard_normal(out[name].shape)
        drawn = base * np.exp(spread * noise) if base else spread * noise
        out[name] = __import__('jax').numpy.asarray(drawn.astype(out[name].dtype))
    for name, factor in factors.items():
        out[name] = (out[name] * factor).astype(out[name].dtype)
    return out
```

```python
from contextlib import ExitStack

import numpy as np
import concourse.bass as bass
from concourse import mybir

ALU = mybir.AluOpType
ACT = mybir.ActivationFunctionType
F32 = mybir.dt.float32
F32R = mybir.dt.float32r
AX = mybir.AxisListType.X

D, DEPTH, SEQ, META = 1024, 2, 256, 16
KC = D // 128
TOK2 = SEQ + META
FF = 4 * D
EPS = 1e-6
NEG = -1e30

UNIT = 2048
NRAW, NSPL = 3, 3
UNITS = 72
LAYERS = 2 * DEPTH
TO_DVE = 1152

GB = (0, 1, 2)
SB_, TB_, YB_ = 3, 5, 7

PE, SC, VE, PO = "tensor", "scalar", "vector", "gpsimd"


def const_tables():
    c = {}
    i = np.arange(128)
    c["ident"] = np.eye(128)
    c["ones"] = np.ones((128, 128))
    c["blk64"] = (i[:, None] // 64 == i[None, :] // 64) * 1.0
    c["causal_neg"] = np.where(i[None, :] <= i[:, None], 0.0, NEG)
    c["strict_neg"] = np.where(i[:, None] < i[None, :], 0.0, NEG)
    c["strict_01"] = (i[:, None] < i[None, :]) * 1.0
    c["suffix"] = np.where(i[:, None] >= i[None, :], -1.0, 0.0)
    c["minus"] = -np.ones((128, 128))

    def rotation(size, half, first):
        r = np.zeros((128, 128))
        for base in range(first, size, 2 * half):
            for a in range(half):
                r[base + half + a, base + a] = -1.0
                r[base + a, base + half + a] = 1.0
        return r

    c["rot_ret"] = rotation(128, 64, 0)
    c["rot_diff"] = rotation(128, 32, 0)
    c["rot_mla"] = rotation(96, 16, 64)
    f32 = np.float32
    inv = f32(10000.0) ** (-np.arange(64, dtype=f32) / f32(64))
    ang = (np.arange(SEQ, dtype=f32)[:, None] * inv[None, :]).astype(f32)
    c["cos_ret"] = np.tile(np.cos(ang).T, (2, 1))
    c["sin_ret"] = np.tile(np.sin(ang).T, (2, 1))
    pos = np.arange(TOK2, dtype=f32)

    def angles(d):
        inv = np.exp(f32(-np.log(10000.0)) * (f32(2.0) * np.arange(d // 2, dtype=f32) / f32(d)))
        return (pos[:, None] * inv[None, :].astype(f32)).astype(f32)

    a = angles(64)
    c["cos_diff"] = np.tile(np.cos(a).T, (4, 1))
    c["sin_diff"] = np.tile(np.sin(a).T, (4, 1))
    a = angles(32)
    cm, sm = np.ones((128, TOK2)), np.zeros((128, TOK2))
    cm[64:96] = np.tile(np.cos(a).T, (2, 1))
    sm[64:96] = np.tile(np.sin(a).T, (2, 1))
    c["cos_mla"], c["sin_mla"] = cm, sm
    dec = []
    for h in range(4):
        lg = np.log(1.0 - 2.0 ** (-5.0 - h))
        n = np.arange(SEQ)
        diff = n[None, :] - i[:, None]
        first = np.where(diff >= 0, np.exp(lg * np.maximum(diff, 0)), 0.0) * 128 ** -0.5
        dec.append(np.concatenate([first, first[:, :128]], axis=1))
    c["decay"] = np.concatenate(dec, axis=1)
    q = np.arange(SEQ).reshape(2, 128).T
    ok = (16 * np.arange(16) + 31)[None, None, :] <= q[:, :, None]
    c["cmp_neg"] = np.where(ok, 0.0, NEG).reshape(128, 32)
    c["cmp_01"] = (ok * 1.0).reshape(128, 32)
    c["eps"] = np.full((128, 1), EPS)
    c["eps64"], c["eps96"] = np.full((128, 1), 64 * EPS), np.full((128, 1), 96 * EPS)
    order = [*BOTH, *FIRST, *(k for k in c if k not in BOTH + FIRST)]
    return {k: np.ascontiguousarray(c[k], dtype=np.float32) for k in order}


def offsets(sizes):
    at, out = 0, {}
    for name, n in sizes:
        out[name] = (at, n)
        at += n
    return out, at


BOTH = ("ident", "ones", "blk64", "causal_neg", "eps", "eps64", "eps96")
FIRST = ("rot_ret", "cos_ret", "sin_ret", "decay", "cmp_neg", "cmp_01")


def const_places(tables):
    sizes = lambda names: [(k, tables[k].shape[1]) for k in names]
    both, own = offsets(sizes(BOTH))
    first, n1 = offsets(sizes(FIRST))
    second, n2 = offsets(sizes([k for k in tables if k not in BOTH + FIRST]))
    at = dict(both)
    at.update({k: (own + a, n) for k, (a, n) in {**first, **second}.items()})
    return at, own, n1, n2


PARAMS1 = [("g_mix", 8), ("g_mlp", 8), ("g_ple", 8), ("g_q", 1), ("g_k", 1), ("pos_k", 16), ("pos_v", 16),
           ("w2_k", 128), ("w2_v", 128), ("p", 2 * SEQ)]
PARAMS2 = [("g_ln1", 8), ("g_ln2", 8), ("g_cq", 2), ("g_ckv", 1), ("g_q", 1), ("g_k", 1), ("g_dq", 1),
           ("g_dk", 1), ("g_do", 1), ("lam", 4), ("lam_init", 1), ("one_less", 1), ("gate_b", 24)]


class Progress:

    def __init__(self, nc, sems):
        self.engines = {PE: nc.tensor, SC: nc.scalar, VE: nc.vector, PO: nc.gpsimd}
        self.sems = sems
        self.restart()

    def restart(self):
        self.count = {e: 0 for e in self.engines}
        self.seen = {}

    def wait(self, engine, *tokens):
        for t in tokens:
            if isinstance(t, list):
                self.wait(engine, *t)
            elif t is not None and self.seen.get((engine, t[0]), 0) < t[1]:
                self.engines[engine].wait_ge(self.sems[t[0]], t[1])
                self.seen[engine, t[0]] = t[1]

    def mark(self, engine, instruction):
        self.count[engine] += 1
        instruction.then_inc(self.sems[engine], 1)
        return (engine, self.count[engine])

    def on(self, engine, *tokens):
        self.wait(engine, *tokens)
        return lambda build, *a, **k: self.mark(engine, build(*a, **k))

    def now(self, *engines):
        return [(e, self.count[e]) for e in engines if self.count[e]]


class Stream:

    def __init__(self, nc, prog, enter):
        self.nc, self.prog = nc, prog
        self.raw = enter(nc.sbuf_tensor("raw_units", [128, NRAW, UNIT], F32))
        self.hi = enter(nc.sbuf_tensor("units_hi", [128, NSPL, UNIT], F32R))
        self.lo = enter(nc.sbuf_tensor("units_lo", [128, NSPL, UNIT], F32R))
        self.landed = [enter(nc.semaphore(f"landed_{s}")) for s in range(NRAW)]
        self.hi_made = [enter(nc.semaphore(f"hi_made_{s}")) for s in range(NSPL)]
        self.lo_made = {e: [enter(nc.semaphore(f"lo_made_{e}_{s}")) for s in range(NSPL)] for e in (VE, PO)}

    def load_all(self, stream):
        sp, body = self.nc.sync, NRAW * NSPL

        def load(i, n):
            back = n - NRAW
            if not isinstance(i, int) or back >= 0:
                turn = i * (body // NSPL) + (back // NSPL + 1)
                for e in (VE, PO):
                    sp.wait_ge(self.lo_made[e][back % NSPL], turn)
            src = stream[bass.ds(i * body + n, 1)].rearrange("a p n -> (a p) n")
            sp.dma_start(self.raw[:, n % NRAW, :], src).then_inc(self.landed[n % NRAW], 16)

        for n in range(body):
            load(0, n)
        with sp.Fori(1, LAYERS * UNITS // body) as i:
            for n in range(body):
                load(i, n)

    def start_layer(self, layer, columns):
        self.layer, self.columns = layer, columns
        self.used, self.next, self.seen = {}, 0, {}
        for _ in range(NSPL - 1):
            self.split_next()

    def split_next(self):
        u = self.next
        if u >= UNITS:
            return
        self.next += 1
        nc, prog, r, s, n = self.nc, self.prog, u % NRAW, u % NSPL, self.columns[u]
        freed = self.used.get(u - NSPL)
        prog.wait(SC, freed)
        nc.scalar.wait_ge(self.landed[r], (self.layer * (UNITS // NRAW) + (u // NRAW + 1)) * 16)
        nc.scalar.activation(self.hi[:, s, :n], self.raw[:, r, :n], ACT.Copy).then_inc(self.hi_made[s], 1)
        cut = n * TO_DVE // UNIT // 2 * 2
        for e, a, b in ((VE, 0, cut), (PO, cut, n)):
            eng = prog.engines[e]
            prog.wait(e, freed)
            eng.wait_ge(self.hi_made[s], self.layer * (UNITS // NSPL) + (u // NSPL + 1))
            eng.tensor_tensor(self.lo[:, s, a:b], self.raw[:, r, a:b], self.hi[:, s, a:b].bitcast(F32),
                              ALU.subtract).then_inc(self.lo_made[e][s], 1)

    def need(self, u, part):
        if self.seen.get((u, part)):
            return
        self.seen[u, part] = True
        turn = self.layer * (UNITS // NSPL) + (u // NSPL + 1)
        sems = [self.hi_made[u % NSPL]] if part == "hi" else [self.lo_made[e][u % NSPL] for e in (VE, PO)]
        for sem in sems:
            self.nc.tensor.wait_ge(sem, turn)

    def view(self, u, kcs):
        n = self.columns[u]
        return [t[:, u % NSPL, :n].rearrange("p (k c) -> p k c", k=kcs) for t in (self.hi, self.lo)]

    def product(self, u, out, pairs, start=True, stop=True, late=(), lows=()):
        nc, prog = self.nc, self.prog
        self.need(u, "hi")
        todo = []
        for part in range(3):
            for k, (a, b, w_first) in enumerate(pairs):
                wl, xl = (0, 1)[part == 1], (0, 1)[part == 2]
                al, bl = (wl, xl) if w_first else (xl, wl)
                todo.append((part, k, a[al], b[bl]))
        for n, (part, k, a, b) in enumerate(todo):
            if part == 0 and lows:
                prog.wait(PE, lows[k])
            if part == 1 and k == 0:
                self.need(u, "lo")
            if part == 2 and k == 0:
                prog.wait(PE, *late)
            m = nc.tensor.matmul(out, a, b, start=start and n == 0, stop=stop and n == len(todo) - 1,
                                 skip_group_check=True)
        t = prog.mark(PE, m)
        self.used[u] = t
        return t


def build(nc, ins, out):
    with ExitStack() as ctx:
        _build(nc, ins, out, ctx.enter_context)


def _build(nc, ins, out, enter):
    tables = const_tables()
    at_const, own0, n1, n2 = const_places(tables)
    n_const = own0 + max(n1, n2)
    at_par1, n_par1 = offsets(PARAMS1)
    at_par2, n_par2 = offsets(PARAMS2)

    prog = Progress(nc, {e: enter(nc.semaphore(f"done_{e}")) for e in (PE, SC, VE, PO)})
    on = prog.on
    loaded = enter(nc.semaphore("loaded"))
    stream = Stream(nc, prog, enter)
    stored = enter(nc.semaphore("stored"))

    def sbuf(name, *shape, dt=F32, into=enter):
        return into(nc.sbuf_tensor(name, list(shape), dt))

    ps = enter(nc.psum_tensor("ps", [128, 8, 512], F32))
    consts = sbuf("consts", 128, n_const)
    x = sbuf("x_res", 128, KC, TOK2)
    h_hi, h_lo = (sbuf(f"h_{n}", 128, KC, TOK2, dt=F32R) for n in ("hi", "lo"))
    sq = sbuf("sq", 128, 2, 512)
    tmp = sbuf("tmp", 128, 2, TOK2)
    rs = sbuf("rs", 128, TOK2)
    params = sbuf("params", 128, max(n_par1, n_par2))

    def C(name, parts=slice(0, 128)):
        a, n = at_const[name]
        return consts[parts, a:a + n]

    def P1(name):
        a, n = at_par1[name]
        return params[:, a:a + n]

    def P2(name, parts=slice(0, 128)):
        a, n = at_par2[name]
        return params[parts, a:a + n]

    free = {b: None for b in range(8)}
    state = {"bank": 0, "filler": None}

    def next_bank():
        b = GB[state["bank"] % len(GB)]
        state["bank"] += 1
        return b

    def fill(n=1):
        for _ in range(n):
            if state["filler"] is not None and next(state["filler"], "end") == "end":
                state["filler"] = None

    def finish_filler():
        while state["filler"] is not None:
            fill()

    def split(src, hi, lo, *after, low_on=PO):
        th = on(SC, *after)(nc.scalar.activation, hi, src, ACT.Copy)
        e = prog.engines[low_on]
        tl = on(low_on, th, *after)(e.tensor_tensor, lo, src, hi.bitcast(F32), ALU.subtract)
        return th, tl

    def inverse_rms(dst, sums, dim, factor, *after):
        parts = sums.shape[0]
        bias = C("eps" if factor == 1 else f"eps{factor}", slice(0, parts))
        t = on(SC, *after)(nc.scalar.activation, dst, sums, ACT.Ln, bias=bias, scale=factor / dim)
        return on(SC, t)(nc.scalar.activation, dst, dst, ACT.Exp, scale=-0.5)

    def rmsnorm(nt, gain, x_done, h_free):
        b, t_sq, t_mm = TB_, [None, None], [None, None]
        prog.wait(PE, free[b])
        for k in range(KC):
            s = k % 2
            t_sq[s] = on(SC, t_mm[s], *x_done)(nc.scalar.activation, sq[:, s, :nt], x[:, k, TOK2 - nt:], ACT.Square)
            t_mm[s] = on(PE, t_sq[s])(nc.tensor.matmul, ps[:, b, :nt], C("ones"), sq[:, s, :nt],
                                      start=k == 0, stop=k == KC - 1)
        t_rs = inverse_rms(rs[:, :nt], ps[:, b, :nt], D, 1, t_mm[1])
        free[b] = t_rs
        his, lows, read = [], [], [None, None]
        for k in range(KC):
            s = k % 2
            t = on(VE, t_rs, read[s])(nc.vector.scalar_tensor_tensor, tmp[:, s, :nt], x[:, k, TOK2 - nt:],
                                      gain[:, k:k + 1], rs[:, :nt], ALU.mult, ALU.mult)
            prog.wait(SC, *h_free)
            prog.wait(PO, *h_free)
            th, tl = split(tmp[:, s, :nt], h_hi[:, k, :nt], h_lo[:, k, :nt], t)
            read[s] = [th, tl]
            his.append(th)
            lows.append(tl)
        return his, lows

    def project(u, kcs, act, nt, evacuate, his=(), lows=(), k0=0, width=128, fillers=1):
        w_hi, w_lo = stream.view(u, kcs)
        for c in range(w_hi.shape[2] // width):
            b = next_bank()
            prog.wait(PE, free[b])
            cols = slice(c * width, (c + 1) * width)
            t = stream.product(u, ps[:, b, :nt],
                               [((w_hi[:, k, cols], w_lo[:, k, cols]),
                                 (act[0][:, k0 + k, :nt], act[1][:, k0 + k, :nt]), True) for k in range(kcs)],
                               late=lows, lows=his)
            if c == 0:
                stream.split_next()
            free[b] = evacuate(c, b, t)
            fill(fillers)

    def project_tokens(u, kcs, act, tiles, cols, evacuate, his=(), lows=()):
        w_hi, w_lo = stream.view(u, kcs)

        for n, (a, m) in enumerate(tiles):
            b = next_bank()
            prog.wait(PE, free[b])
            t = stream.product(u, ps[:, b, :cols],
                               [((act[0][:, k, a:a + 128], act[1][:, k, a:a + 128]),
                                 (w_hi[:, k, :cols], w_lo[:, k, :cols]), False) for k in range(kcs)],
                               late=lows, lows=his)
            if n == 0:
                stream.split_next()
            free[b] = evacuate(n, b, t)
            fill()

    def copy_to(dst, engine=SC, *more):
        def evacuate(c, b, t):
            d = dst(c)
            src = ps[:d.shape[0], b, :]
            src = src[:, :d.free_size()] if len(d.shape) == 2 else src[:, :d.free_size()]
            if engine == SC:
                return on(SC, t, *more)(nc.scalar.activation, d, src, ACT.Copy)
            return on(VE, t, *more)(nc.vector.tensor_copy, d, src)
        return evacuate

    def add_to_residual(nt, first, done):
        def evacuate(c, b, t):
            k = first + c
            tok = on(VE, t)(nc.vector.tensor_tensor, x[:, k, TOK2 - nt:], x[:, k, TOK2 - nt:], ps[:, b, :nt], ALU.add)
            done.append(tok)
            return tok
        return evacuate

    def mlp(u, nt, his, lows, into, name):
        with ExitStack() as own:
            f_hi, f_lo = (sbuf(f"{name}_ff_{n}", 128, FF // 128, nt, dt=F32R, into=own.enter_context)
                          for n in ("hi", "lo"))
            gone = prog.now(PE, SC, VE, PO)
            for e in (SC, VE, PO):
                prog.wait(e, gone)
            read, f_his, f_lows = [None, None], [], []
            for n in range(16):
                def evacuate(c, b, t, n=n):
                    s, k = (2 * n + c) % 2, 2 * n + c
                    r = tmp[:, s, :nt]
                    t1 = on(SC, t, read[s])(nc.scalar.activation, r, ps[:, b, :nt], ACT.Relu)
                    t2 = on(VE, t1)(nc.vector.tensor_tensor, r, r, r, ALU.mult)
                    th, tl = split(r, f_hi[:, k, :], f_lo[:, k, :], t2, low_on=VE)
                    read[s] = [th, tl]
                    f_his.append(th)
                    f_lows.append(tl)
                    return t1
                project(u + n, KC, (h_hi, h_lo), nt, evacuate, his, lows)
            u += 16
            done = []
            for pair in range(4):
                banks = [next_bank(), next_bank()]
                for kb in range(4):
                    w = stream.view(u, KC)
                    for c, b in enumerate(banks):
                        if kb == 0:
                            prog.wait(PE, free[b])
                        cols = slice(c * 128, (c + 1) * 128)
                        ks = range(kb * KC, (kb + 1) * KC)
                        t = stream.product(u, ps[:, b, :nt],
                                           [((w[0][:, k - kb * KC, cols], w[1][:, k - kb * KC, cols]),
                                             (f_hi[:, k, :], f_lo[:, k, :]), True) for k in ks],
                                           start=kb == 0, stop=kb == 3, late=[f_lows[ks[-1]]],
                                           lows=[f_his[k] for k in ks])
                        if c == 0:
                            stream.split_next()
                        if kb == 3:
                            free[b] = add_to_residual(nt, 2 * pair, done)(c, b, t)
                    u += 1
        return u, done

    def pipeline(items, scores, turn, apply):
        for k in range(len(items) + 2):
            if k >= 2:
                apply(items[k - 2])
            if k < len(items):
                scores(items[k])
            if 1 <= k <= len(items):
                turn(items[k - 1])
            yield

    COLS1 = [2048] * UNITS
    COLS1[6] = KC * 24

    def nsa_attention(B, t_in, t_gate, t_hid, ready):
        zq, zk, vtok, gate, hid = B["zq"], B["zk"], B["vtok"], B["gate"], B["hid"]
        t_norm, before = {}, []
        for name, view, gain, factor, src in (("q01", zq[:, 0:2, :], "g_q", 64, t_in["q"]),
                                              ("q23", zq[:, 2:4, :], "g_q", 64, t_in["q"]),
                                              ("k", zk[:, :, :], "g_k", 1, t_in["k"])):
            flat = view.rearrange("p a t -> p (a t)")
            s = on(SC, *src, *before)(nc.scalar.activation, sq[:, 0, :], flat, ACT.Square)
            yield
            m = on(PE, s, free[TB_])(nc.tensor.matmul, ps[:, TB_, :], C("blk64"), sq[:, 0, :], start=True, stop=True)
            r = inverse_rms(B["rn"][:, :], ps[:, TB_, :], 64, factor, m)
            free[TB_] = r
            t_norm[name] = on(VE, r)(nc.vector.scalar_tensor_tensor, flat, flat, P1(gain), B["rn"][:, :],
                                     ALU.mult, ALU.mult)
            before = [m, t_norm[name]]
            yield
        kc_ps, vc_ps = ps[:, TB_, 0:16], ps[0:16, TB_ + 1, 0:128]
        prog.wait(PE, free[TB_], free[TB_ + 1], *t_hid)
        for g in range(2):
            rows = slice(64 * g, 64 * g + 64)
            for hc in range(2):
                m = nc.tensor.matmul(kc_ps[rows, :], P1("w2_k")[:, hc * 64:hc * 64 + 64],
                                     hid[:, 0, hc, 16 * g:16 * g + 16], start=hc == 0, stop=hc == 1)
        t_k = prog.mark(PE, m)
        for g in range(2):
            for hc in range(2):
                m = nc.tensor.matmul(vc_ps[:, 64 * g:64 * g + 64], hid[:, 1, hc, 16 * g:16 * g + 16],
                                     P1("w2_v")[:, hc * 64:hc * 64 + 64], start=hc == 0, stop=hc == 1)
        t_v = prog.mark(PE, m)
        kcmp, vcmp = B["kcmp"], B["vcmp"]
        t1 = on(SC, t_k)(nc.scalar.activation, sq[:, 0, :16], kc_ps, ACT.Square)
        t2 = on(SC, t_k)(nc.scalar.activation, kcmp[:, :], kc_ps, ACT.Copy)
        t_vc = on(SC, t_v)(nc.scalar.activation, vcmp[:, :], vc_ps, ACT.Copy)
        free[TB_], free[TB_ + 1] = t2, t_vc
        yield
        m = on(PE, t1, t2)(nc.tensor.matmul, ps[:, TB_, :16], C("blk64"), sq[:, 0, :16], start=True, stop=True)
        r = inverse_rms(B["rn"][:, :16], ps[:, TB_, :16], 64, 1, m, *t_norm.values())
        free[TB_] = r
        t_kc = on(VE, r)(nc.vector.scalar_tensor_tensor, kcmp[:, :], kcmp[:, :], P1("g_k"), B["rn"][:, :16],
                         ALU.mult, ALU.mult)
        yield

        small = B["small"]
        turned = {"pt": None, "e": [None, None]}
        items = []
        for t in range(2):
            items.append({"t": t, "kind": "cmp"})
            items += [{"t": t, "kind": "keys", "br": br, "g": g} for br in range(2) for g in range(2)]
        for n, it in enumerate(items):
            it["n"] = n
        y_started = {}

        def scores(it):
            t, n = it["t"], it["n"]
            e = B["e"][:, n % 2, :]
            nm, sm, f = (small[:, n % 2, a, :] for a in range(3))
            prog.wait(PE, free[SB_], *t_norm.values(), t_kc)
            if it["kind"] == "cmp":
                s = ps[:, SB_:SB_ + 2, 0:64].rearrange("p g (j n) -> p g j n", j=4)
                for g in range(2):
                    rows = slice(64 * g, 64 * g + 64)
                    for j in range(4):
                        m = nc.tensor.matmul(s[:, g, j, :], zq[rows, j, 128 * t:128 * t + 128], kcmp[rows, :],
                                             start=True, stop=True)
                m = prog.mark(PE, m)
                ev = e[:, :128].rearrange("p (h n) -> p h n", h=8)
                neg = C("cmp_neg")[:, 16 * t:16 * t + 16].unsqueeze(1).unsqueeze(1).to_broadcast([128, 2, 4, 16])
                ok = C("cmp_01")[:, 16 * t:16 * t + 16].unsqueeze(1).to_broadcast([128, 8, 16])
                a = on(VE, m, turned["e"][n % 2])(nc.vector.tensor_tensor, e[:, :128].rearrange(
                    "p (g j n) -> p g j n", g=2, j=4), s, neg, ALU.add)
                free[SB_] = a
                a = on(VE, a)(nc.vector.reduce_max, nm, ev, AX, negate=True)
                a = on(VE, a)(nc.vector.tensor_tensor, ev, ev, nm.unsqueeze(2).to_broadcast([128, 8, 16]), ALU.add)
                a = on(SC, a)(nc.scalar.activation, e[:, :128], e[:, :128], ACT.Exp)
                a = on(VE, a)(nc.vector.tensor_tensor, ev, ev, ok, ALU.mult)
                a = on(VE, a)(nc.vector.reduce_sum, sm, ev, AX)
                a = on(VE, a)(nc.vector.tensor_scalar, sm, sm, 1e-30, None, ALU.max)
                a = on(VE, a)(nc.vector.reciprocal, f, sm)
                a = on(VE, a, t_gate)(nc.vector.tensor_tensor, f, f, gate[:, t, 0:8], ALU.mult)
                it["p"] = on(VE, a)(nc.vector.tensor_tensor, ev, ev, f.unsqueeze(2).to_broadcast([128, 8, 16]), ALU.mult)
                return
            L, br, g = 128 * (t + 1), it["br"], it["g"]
            rows = slice(64 * g, 64 * g + 64)
            s = ps[:, SB_:SB_ + 2, :].rearrange("p b c -> p (b c)")[:, :4 * L].rearrange("p (j l) -> p j l", j=4)
            for j in range(4):
                nc.tensor.matmul(s[:, j, :], zq[rows, j, 128 * t:128 * t + 128], zk[rows, br, :L], start=True, stop=False)
                m = nc.tensor.matmul(s[:, j, L - 128:], C("ident"), C("causal_neg"), start=False, stop=True)
            m = prog.mark(PE, m)
            a = on(VE, m)(nc.vector.reduce_max, nm[:, :4], s, AX, negate=True)
            ev = e[:, :4 * L].rearrange("p (j l) -> p j l", j=4)
            prog.wait(SC, a, turned["e"][n % 2])
            for j in range(4):
                b = on(SC)(nc.scalar.activation, ev[:, j, :], s[:, j, :], ACT.Exp, bias=nm[:, j:j + 1],
                           accum_out=sm[:, j:j + 1])
            free[SB_] = [a, b]
            a = on(VE, b)(nc.vector.reciprocal, f[:, :4], sm[:, :4])
            c0 = (1 + br) * 8 + 4 * g
            a = on(VE, a, t_gate)(nc.vector.tensor_tensor, f[:, :4], f[:, :4], gate[:, t, c0:c0 + 4], ALU.mult)
            it["p"] = on(VE, a)(nc.vector.tensor_tensor, ev, ev, f[:, :4].unsqueeze(2).to_broadcast([128, 4, L]), ALU.mult)

        def turn(it):
            n, t = it["n"], it["t"]
            e, pt = B["e"][:, n % 2, :], B["pt"]
            prog.wait(PE, it["p"], free[TB_], free[TB_ + 1])
            if it["kind"] == "cmp":
                for h in range(8):
                    m = nc.tensor.transpose(ps[:16, TB_ + h // 4, h % 4 * 128:h % 4 * 128 + 128],
                                            e[:, 16 * h:16 * h + 16], C("ident"))
                m = prog.mark(PE, m)
                it["pt"] = on(VE, m, turned["pt"])(nc.vector.tensor_copy, pt[:16, :, :], ps[:16, TB_:TB_ + 2, :])
                free[TB_] = free[TB_ + 1] = it["pt"]
            else:
                L = 128 * (t + 1)
                ev = e[:, :4 * L].rearrange("p (j l) -> p j l", j=4)
                done = []
                for kc in range(t + 1):
                    for j in range(4):
                        m = nc.tensor.transpose(ps[:, TB_ + kc, 128 * j:128 * j + 128],
                                                ev[:, j, 128 * kc:128 * kc + 128], C("ident"))
                    m = prog.mark(PE, m)
                    c = on(VE, m, turned["pt"])(nc.vector.tensor_copy, pt[:, kc, :], ps[:, TB_ + kc, :])
                    free[TB_ + kc] = c
                    done.append(c)
                it["pt"] = done
            turned["e"][n % 2] = m

        def apply(it):
            t, pt = it["t"], B["pt"]
            prog.wait(PE, it["pt"], t_vc, t_in["v"])
            if it["kind"] == "cmp":
                prog.wait(PE, free[YB_])
                for g in range(2):
                    m = nc.tensor.matmul(ps[64 * g:64 * g + 64, YB_, :], vcmp[:, 64 * g:64 * g + 64], pt[:16, g, :],
                                         start=True, stop=True, skip_group_check=True)
            else:
                br, g = it["br"], it["g"]
                for kc in range(t + 1):
                    v = vtok[:, kc, 128 * br + 64 * g:128 * br + 64 * g + 64]
                    m = nc.tensor.matmul(ps[64 * g:64 * g + 64, YB_, :], v, pt[:, kc, :], start=False,
                                         stop=True, skip_group_check=True)
            m = turned["pt"] = prog.mark(PE, m)
            if it["kind"] == "keys" and it["br"] == 1 and it["g"] == 1:
                y = B["yn"][:, :, 128 * t:128 * t + 128]
                c = on(SC, m)(nc.scalar.activation, y, ps[:, YB_, :].rearrange("p (j q) -> p j q", j=4), ACT.Copy)
                free[YB_] = c
                th, tl = split(y, B["yn_hi"][:, :, 128 * t:128 * t + 128], B["yn_lo"][:, :, 128 * t:128 * t + 128], c)
                B["yn_hi_done"].append(th)
                B["yn_lo_done"].append(tl)

        yield from pipeline(items, scores, turn, apply)
        while not ready["ret"]:
            yield
        yield from retention(B)

    def retention(B):
        rq, rk, rv, yr, rot = B["rq"], B["rk"], B["rv"], B["yr"], B["rot"]
        t_rope = []
        for r in (rq, rk):
            for pair in range(2):
                v = r[:, 2 * pair:2 * pair + 2, :]
                cos, sin = (C(c).unsqueeze(1).to_broadcast([128, 2, SEQ]) for c in ("cos_ret", "sin_ret"))
                m = on(PE, free[TB_], B["t_r"])(nc.tensor.matmul, ps[:, TB_, :], C("rot_ret"),
                                               v.rearrange("p a t -> p (a t)"), start=True, stop=True)
                a = on(VE, m, *t_rope[-1:])(nc.vector.tensor_tensor, rot[:, :, :],
                                            ps[:, TB_, :].rearrange("p (a t) -> p a t", a=2), sin, ALU.mult)
                free[TB_] = a
                b = on(VE, m)(nc.vector.tensor_tensor, v, v, cos, ALU.mult)
                t_rope.append(on(VE, a, b)(nc.vector.tensor_tensor, v, v, rot[:, :, :], ALU.add))
                yield
        read = [None, None]

        def scores(h):
            prog.wait(PE, free[SB_], *t_rope)
            nc.tensor.matmul(ps[:, SB_, 0:256], rk[:, h, 0:128], rq[:, h, :], start=True, stop=True)
            m = on(PE)(nc.tensor.matmul, ps[:, SB_, 256:384], rk[:, h, 128:256], rq[:, h, 128:256], start=True, stop=True)
            B[f"a{h}"] = on(VE, m, read[h % 2])(nc.vector.tensor_tensor, B["e"][:, h % 2, :384], ps[:, SB_, :384],
                                               C("decay")[:, 384 * h:384 * h + 384], ALU.mult)
            free[SB_] = B[f"a{h}"]

        def turn(h):
            a, e = slice(128 * h, 128 * h + 128), B["e"][:, h % 2, :]
            prog.wait(PE, free[YB_], B[f"a{h}"], *B["t_rv"])
            nc.tensor.matmul(ps[:, YB_, :256], rv[:, 0, a], e[:, 0:256], start=True, stop=True, skip_group_check=True)
            m = on(PE)(nc.tensor.matmul, ps[:, YB_, 128:256], rv[:, 1, a], e[:, 256:384], start=False, stop=True,
                       skip_group_check=True)
            read[h % 2] = m
            c = on(SC, m)(nc.scalar.activation, yr[:, h, :], ps[:, YB_, :256], ACT.Copy)
            free[YB_] = B[f"y{h}"] = on(SC, c, B.get(f"m{h - 2}"))(nc.scalar.activation, sq[:, h % 2, :256], ps[:, YB_, :256], ACT.Square)

        def apply(h):
            m = B[f"m{h}"] = on(PE, free[TB_], B[f"y{h}"])(nc.tensor.matmul, ps[:, TB_, :256], C("ones"), sq[:, h % 2, :256],
                                                          start=True, stop=True)
            r = inverse_rms(B["rn"][:, :256], ps[:, TB_, :256], 128, 1, m, *B["yr_done"][-1:])
            free[TB_] = r
            B["yr_done"].append(on(VE, r)(nc.vector.tensor_tensor, yr[:, h, :], yr[:, h, :], B["rn"][:, :256], ALU.mult))

        yield from pipeline(list(range(4)), scores, turn, apply)

    def first_layer(i):
        nt = SEQ
        stream.start_layer(i, COLS1)
        nc.scalar.dma_start(params[:, :n_par1], ins["params1"][bass.ds(i, 1)].rearrange("a p n -> (a p) n"))\
            .then_inc(loaded, 16)
        for e in (SC, VE, PE):
            prog.engines[e].wait_ge(loaded, 16)
        his, lows = rmsnorm(nt, P1("g_mix"), [], [])
        act = (h_hi, h_lo)
        with ExitStack() as own:
            keep = own.enter_context

            def buf(name, *shape, dt=F32, into=keep):
                return sbuf("b1_" + name, 128, *shape, dt=dt, into=into)

            B = {"zq": buf("zq", 4, nt), "zk": buf("zk", 2, nt), "vtok": buf("vtok", 2, 256),
                 "gate": buf("gate", 2, 24), "e": buf("e", 2, 1024), "pt": buf("pt", 2, 512),
                 "small": buf("small", 2, 3, 8), "rn": buf("rn", 512), "rot": buf("rot", 2, nt),
                 "hid": buf("hid", 2, 2, 32), "kcmp": buf("kcmp", 16),
                 "vcmp": sbuf("b1_vcmp", 16, 128, into=keep), "yn": buf("yn", 4, nt),
                 "yn_hi": buf("yn_hi", 4, nt, dt=F32R), "yn_lo": buf("yn_lo", 4, nt, dt=F32R),
                 "rq": buf("rq", 4, nt), "rk": buf("rk", 4, nt), "rv": buf("rv", 2, 512),
                 "rg": buf("rg", 4, nt), "yr": buf("yr", 4, nt),
                 "yn_hi_done": [], "yn_lo_done": [], "yr_done": [], "t_rv": []}
            inner = ExitStack()
            shifted = buf("shifted", 4, nt + 16, into=inner.enter_context)
            z32 = buf("z32", 2, 512, into=inner.enter_context)
            z_hi, z_lo = (buf(f"z_{n}", 2, 512, dt=F32R, into=inner.enter_context) for n in ("hi", "lo"))
            z_done = []
            for kv in range(2):
                built = []

                def evacuate(g, b, t, kv=kv, built=built):
                    s = shifted[:, 2 * kv + g, :]
                    on(SC, t)(nc.scalar.activation, s[0:64, 0:nt], ps[0:64, b, 0:nt], ACT.Copy)
                    on(SC)(nc.scalar.activation, s[64:128, 0:nt - 1], ps[64:128, b, 1:nt], ACT.Copy)
                    last = ps[:, b, nt - 1:nt]
                    on(SC)(nc.scalar.activation, s[0:64, nt:nt + 16], last[0:64, :].to_broadcast([64, 16]), ACT.Copy)
                    c = on(SC)(nc.scalar.activation, s[64:128, nt - 1:nt + 16],
                               last[64:128, :].to_broadcast([64, 17]), ACT.Copy)
                    out_ = z32[:, kv, :].rearrange("p (c g n) -> p c g n", c=16, g=2)
                    for half in range(2):
                        src = s[:, 16 * half:16 * half + nt].rearrange("p (n c two) -> p c n two", c=8, two=2)[:, :, :, 0]
                        pos = P1("pos_k" if kv == 0 else "pos_v")[:, 8 * half:8 * half + 8]
                        built.append(on(VE, c)(nc.vector.tensor_tensor, out_[:, 8 * half:8 * half + 8, g, :], src,
                                                  pos.unsqueeze(2).to_broadcast([128, 8, 16]), ALU.add))
                    return c

                project(kv, KC, act, nt, evacuate, his, lows)
                z_done.append(split(z32[:, kv, :], z_hi[:, kv, :], z_lo[:, kv, :], *built))
            t_in = {"q": [], "k": [], "v": []}

            def track(evacuate, into):
                def wrapped(c, b, t):
                    tok = evacuate(c, b, t)
                    into.append(tok)
                    return tok
                return wrapped

            for n in range(2):
                project(2 + n, KC, act, nt, track(copy_to(lambda c, n=n: B["zq"][:, 2 * n + c, :]), t_in["q"]))
            project(4, KC, act, nt, track(copy_to(lambda c: B["zk"][:, c, :]), t_in["k"]))
            tiles = [(0, 128), (128, 128)]
            project_tokens(5, KC, act, tiles, 256, track(copy_to(lambda c: B["vtok"][:, c, :]), t_in["v"]))
            gates = []

            def gate_out(c, b, t):
                g = B["gate"][:, c, :]
                e = on(SC, t)(nc.scalar.activation, g, ps[:, b, 0:24], ACT.Exp, scale=-1.0)
                a = on(VE, e)(nc.vector.tensor_scalar, g, g, 1.0, None, ALU.add)
                gates.append(on(VE, a)(nc.vector.reciprocal, g, g))
                return e
            project_tokens(6, KC, act, tiles, 24, gate_out)
            t_hid = []
            scratch = buf("gelu", 3, 32, into=inner.enter_context)
            for n in range(4):
                kv, hc = divmod(n, 2)
                w_hi, w_lo = stream.view(7 + n, 16)
                b = next_bank()
                prog.wait(PE, free[b])
                zs = [slice(32 * c, 32 * c + 32) for c in range(16)]
                t = stream.product(7 + n, ps[:, b, :32],
                                   [((w_hi[:, c, :], w_lo[:, c, :]), (z_hi[:, kv, zs[c]], z_lo[:, kv, zs[c]]), True)
                                    for c in range(16)], late=[z_done[kv][1]], lows=[z_done[kv][0]] * 16)
                stream.split_next()
                zc, z2, ez = (scratch[:, a, :] for a in range(3))
                prev = t_hid[-1:]
                a = on(SC, t, *prev)(nc.scalar.activation, zc, ps[:, b, :32], ACT.Copy)
                c = on(SC, t, *prev)(nc.scalar.activation, z2, ps[:, b, :32], ACT.Square)
                free[b] = c
                d = on(VE, c)(nc.vector.tensor_scalar, z2, z2, 0.044715, 1.0, ALU.mult, ALU.add)
                d = on(VE, a, d)(nc.vector.tensor_tensor, z2, z2, zc, ALU.mult)
                d = on(SC, d)(nc.scalar.activation, ez, z2, ACT.Exp, scale=-2.0 * float(np.sqrt(2.0 / np.pi)))
                d = on(VE, d)(nc.vector.tensor_scalar, ez, ez, 1.0, None, ALU.add)
                d = on(VE, d)(nc.vector.reciprocal, ez, ez)
                t_hid.append(on(VE, d)(nc.vector.tensor_tensor, B["hid"][:, kv, hc, :], zc, ez, ALU.mult))
            inner.close()
            ready = {"ret": False}
            state["filler"] = nsa_attention(B, t_in, gates[-1], t_hid, ready)
            t_r = []
            for n in range(2):
                project(11 + n, KC, act, nt, track(copy_to(lambda c, n=n: B["rq"][:, 2 * n + c, :]), t_r))
            for n in range(2):
                project(13 + n, KC, act, nt, track(copy_to(lambda c, n=n: B["rk"][:, 2 * n + c, :]), t_r))
            for n in range(2):
                cols = slice(256 * n, 256 * n + 256)
                project_tokens(15 + n, KC, act, tiles, 256,
                               track(copy_to(lambda c, cols=cols: B["rv"][:, c, cols]), B["t_rv"]))
            t_g = []
            for n in range(2):
                project(17 + n, KC, act, nt, track(copy_to(lambda c, n=n: B["rg"][:, 2 * n + c, :]), t_g))
            B["t_r"] = t_r
            ready["ret"] = True
            merge = buf("merge", 16, nt, into=keep)
            prog.wait(SC, prog.now(PE, VE, PO))
            t_m = []
            for n in range(8):
                project(19 + n, KC, act, nt, track(copy_to(lambda c, n=n: merge[:, 2 * n + c, :]), t_m))
            finish_filler()
            sig = B["e"][:, 0, :].rearrange("p (h t) -> p h t", h=4)
            t_s = []
            for n in range(2):
                half = merge[:, 8 * n:8 * n + 8, :].rearrange("p c t -> p (c t)")
                if n == 1:
                    t_rg = on(SC, *t_g, prog.now(PE))(nc.scalar.activation, sig, B["rg"][:, :, :], ACT.Sigmoid)
                t_s.append(on(SC, *t_m)(nc.scalar.activation, half, half, ACT.Sigmoid))
            nc.scalar.preload_act_table_set("natural_log_exp_and_others")
            a = on(VE, t_rg)(nc.vector.tensor_tensor, sig, sig, B["rg"][:, :, :], ALU.mult)
            a = on(VE, a, *B["yr_done"])(nc.vector.tensor_tensor, B["yr"][:, :, :], B["yr"][:, :, :], sig, ALU.mult)
            h_read = prog.now(PE)
            r_his, r_lows = split(B["yr"][:, :, :], h_hi[:, 4:8, :nt], h_lo[:, 4:8, :nt], a, *h_read)

            def merge_nsa(n):
                def evacuate(c, b, t):
                    m = merge[:, 4 * n + c, :]
                    return on(VE, t, t_s[0])(nc.vector.tensor_tensor, m, m, ps[:, b, :nt], ALU.mult)
                return evacuate

            mixed = []

            def merge_ret(n):
                def evacuate(c, b, t):
                    m, r = merge[:, 4 * n + c, :], merge[:, 8 + 4 * n + c, :]
                    a = on(VE, t, t_s[1])(nc.vector.tensor_tensor, r, r, ps[:, b, :nt], ALU.mult)
                    mixed.append(on(PO, a)(nc.gpsimd.tensor_tensor, m, m, r, ALU.add))
                    return a
                return evacuate

            for n in range(2):
                project(27 + n, 4, (B["yn_hi"], B["yn_lo"]), nt, merge_nsa(n), [B["yn_hi_done"]] * 4, B["yn_lo_done"])
            for n in range(2):
                project(29 + n, 4, act, nt, merge_ret(n), [r_his] * 4, [r_lows], k0=4)
            h_read = prog.now(PE)
            his, lows = [], []
            for k in range(KC):
                th, tl = split(merge[:, k, :], h_hi[:, k, :nt], h_lo[:, k, :nt], mixed[k], *h_read,
                               low_on=VE if k % 2 else PO)
                his.append(th)
                lows.append(tl)
            x_done = []
            for n in range(4):
                project(31 + n, KC, act, nt, add_to_residual(nt, 2 * n, x_done), his, lows)
        his, lows = rmsnorm(nt, P1("g_mlp"), x_done, prog.now(PE))
        u, x_done = mlp(35, nt, his, lows, None, "b1")
        with ExitStack() as own:
            ple = sbuf("b1_ple", 128, KC, nt, into=own.enter_context)
            p_hi, p_lo = (sbuf(f"b1_p_{n}", 128, 2, nt, dt=F32R, into=own.enter_context) for n in ("hi", "lo"))
            p = P1("p").rearrange("q (k t) -> q k t", k=2)
            th, tl = split(p, p_hi[:, :, :], p_lo[:, :, :], prog.now(PE, VE, PO))
            t_p = []
            project(u, 2, (p_hi, p_lo), nt, track(copy_to(lambda c: ple[:, c, :], VE), t_p), [th] * 2, [tl])
            u += 1
            his, lows = rmsnorm(nt, P1("g_ple"), x_done, prog.now(PE))
            used = [None, None]

            def gated(n):
                def evacuate(c, b, t):
                    k = 2 * n + c
                    g = tmp[:, k % 2, :nt]
                    a = on(SC, t, used[k % 2], *lows)(nc.scalar.activation, g, ps[:, b, :nt], ACT.Sigmoid)
                    d = on(VE, a, *t_p)(nc.vector.tensor_tensor, g, g, ple[:, k, :], ALU.mult)
                    used[k % 2] = on(VE, d)(nc.vector.tensor_tensor, x[:, k, TOK2 - nt:], x[:, k, TOK2 - nt:], g, ALU.add)
                    return a
                return evacuate

            for n in range(4):
                project(u, KC, act, nt, gated(n), his, lows)
                u += 1
            assert u == UNITS

    COLS2 = [2048] * UNITS
    COLS2[7] = 1024
    COLS2[UNITS - 2:] = [4, 4]

    TILES = [(META, 128), (META + 128, 128), (0, META)]
    SEEN = [[2, 0], [2, 0, 1], [2]]

    def rope_norms(todo, B):
        rn, rot = B["rn"], B["rot"]
        done, last = [], [None, None]
        state_ = {}

        def before(n):
            v, rows, gain, _, _, _, _, toks = todo[n]
            s = n % 2
            a = on(SC, *toks, last[s])(nc.scalar.activation, sq[rows, s, :TOK2], v, ACT.Square)
            g = on(VE, a, *toks)(nc.vector.tensor_scalar, v, v, gain, None, ALU.mult)
            state_[n] = [a, g]

        def after(n):
            v, rows, _, ones, names, dim, factor, _ = todo[n]
            s, b0, b1 = n % 2, TB_, TB_ + 1
            count = rows.stop
            prog.wait(PE, *state_[n], free[b0], free[b1])
            m0 = on(PE)(nc.tensor.matmul, ps[rows, b0, :TOK2], C(ones, rows)[:, :count], sq[rows, s, :TOK2],
                        start=True, stop=True)
            m1 = on(PE)(nc.tensor.matmul, ps[rows, b1, :TOK2], C(names[0], rows)[:, :count], v, start=True, stop=True)
            r = inverse_rms(rn[rows, s, :], ps[rows, b0, :TOK2], dim, factor, m0, last[s])
            a = on(VE, m1, last[s])(nc.vector.tensor_tensor, rot[rows, s, :], ps[rows, b1, :TOK2], C(names[2], rows), ALU.mult)
            free[b0], free[b1] = r, a
            c = on(VE, m1)(nc.vector.tensor_tensor, v, v, C(names[1], rows), ALU.mult)
            a = on(VE, a, c)(nc.vector.tensor_tensor, v, v, rot[rows, s, :], ALU.add)
            last[s] = on(VE, a, r)(nc.vector.tensor_tensor, v, v, rn[rows, s, :], ALU.mult)
            done.append(last[s])

        for n in range(len(todo) + 1):
            if n < len(todo):
                before(n)
            if n >= 1:
                after(n - 1)
            yield done

    def softmax_attention(B, groups, query, key, value, width, combine, finish, toks):
        e, pt, ptm, small = B["e"], B["pt"], B["ptm"], B["small"]
        items = [{"g": g, "t": t} for g in groups for t in (1, 0, 2)]
        for n, it in enumerate(items):
            it["n"] = n
        turned = {"e": [None, None], "pt": None}

        def scores(it):
            g, t, n = it["g"], it["t"], it["n"]
            q0, m = TILES[t]
            L = q0 + m
            prog.wait(PE, free[SB_], *toks)
            for s in range(2):
                q, k = query(g, s)[:, q0:q0 + m], key(g, s)
                bank = ps[:m, SB_ + s, :]
                nc.tensor.matmul(bank[:, :L], q, k[:, :L], start=True, stop=False)
                a = nc.tensor.matmul(bank[:, q0:L], C("ident")[:m, :m], C("causal_neg")[:m, :m], start=False, stop=True)
            a = prog.mark(PE, a)
            S, E = ps[:m, SB_:SB_ + 2, :L], e[:m, n % 2, :, :L]
            nm, sm, f = (small[:m, n % 2, c, :2] for c in range(3))
            a = on(VE, a)(nc.vector.reduce_max, nm, S, AX, negate=True)
            prog.wait(SC, a, turned["e"][n % 2])
            for s in range(2):
                b = on(SC)(nc.scalar.activation, E[:, s, :], S[:, s, :], ACT.Exp, bias=nm[:, s:s + 1],
                           accum_out=sm[:, s:s + 1])
            free[SB_] = [a, b]
            a = on(VE, b)(nc.vector.reciprocal, f, sm)
            it["p"] = combine(E, f, a, m, L)

        def turn(it):
            t, n = it["t"], it["n"]
            m = TILES[t][1]
            prog.wait(PE, it["p"], free[TB_], free[TB_ + 1])
            for s in range(width):
                for kt in SEEN[t]:
                    c0, w = TILES[kt]
                    dst = (ps[:w, TB_ + 1, 128 * s:128 * s + m] if kt == 2
                           else ps[:, TB_, 256 * s + 128 * kt:256 * s + 128 * kt + m])
                    a = nc.tensor.transpose(dst, e[:m, n % 2, s, c0:c0 + w], C("ident")[:m, :m])
            a = turned["e"][n % 2] = prog.mark(PE, a)
            done = []
            if t != 2:
                view = [z.rearrange("p (s k c) -> p s k c", s=2, k=2)[:, :width, :t + 1, :]
                        for z in (pt, ps[:, TB_, :])]
                done.append(on(VE, a, turned["pt"])(nc.vector.tensor_copy, view[0], view[1]))
            view = [z.rearrange("p (s c) -> p s c", s=2)[:, :width, :m] for z in (ptm[:, :], ps[:META, TB_ + 1, :256])]
            done.append(on(SC, a, turned["pt"])(nc.scalar.activation, view[0], view[1], ACT.Copy))
            free[TB_] = free[TB_ + 1] = it["pt"] = done

        def apply(it):
            g, t = it["g"], it["t"]
            q0, m = TILES[t]
            prog.wait(PE, it["pt"])
            if t == 1:
                prog.wait(PE, free[YB_])
            for s in range(width):
                rows = slice(64 * s, 64 * s + 64) if width == 2 else slice(0, 128)
                for c, kt in enumerate(SEEN[t]):
                    p = ptm[:, 128 * s:128 * s + m] if kt == 2 else pt[:, 256 * s + 128 * kt:256 * s + 128 * kt + m]
                    a = nc.tensor.matmul(ps[rows, YB_, q0:q0 + m], value(g, s, kt), p, start=c == 0, stop=True,
                                         skip_group_check=True)
            a = turned["pt"] = prog.mark(PE, a)
            if t == 2:
                free[YB_] = finish(g, a)

        yield from pipeline(items, scores, turn, apply)

    def mla(B, heads, t_v):
        mq, mk, mv, kr, rn = B["mq"], B["mk"], B["mv"], B["kr"], B["rn"]
        rows = slice(0, 96)
        names = ("rot_mla", "cos_mla", "sin_mla")
        todo = [(mq[:96, h, :], rows, P2("g_q", rows), "ones", names, 96, 96, heads["q"]) for h in range(8)]
        up = slice(64, 96)
        a = on(SC, *heads["kr"])(nc.scalar.activation, B["ksq"][up, 0, :], kr[up, :], ACT.Square)
        b = on(SC, a)(nc.scalar.activation, B["ksq"][up, 1, :], kr[up, :], ACT.Square)
        g = on(VE, b)(nc.vector.tensor_scalar, kr[up, :], kr[up, :], P2("g_k", up), None, ALU.mult)
        yield
        m = on(PE, g, free[TB_])(nc.tensor.matmul, ps[:96, TB_, :TOK2], C("rot_mla", up)[:, :96], kr[up, :],
                                 start=True, stop=True)
        a = on(VE, m)(nc.vector.tensor_tensor, B["rot"][up, 0, :], ps[up, TB_, :TOK2], C("sin_mla", up), ALU.mult)
        free[TB_] = a
        c = on(VE, m)(nc.vector.tensor_tensor, kr[up, :], kr[up, :], C("cos_mla", up), ALU.mult)
        roped = on(VE, a, c)(nc.vector.tensor_tensor, kr[up, :], kr[up, :], B["rot"][up, 0, :], ALU.add)
        yield
        ready = []
        for done in rope_norms(todo, B):
            yield
        ready += done[-2:]
        last, squared = [ready, ready], {}
        for n in range(9):
            if n < 8:
                squared[n] = on(SC, last[n % 2], *heads["k"])(nc.scalar.activation, B["ksq"][0:64, n % 2, :],
                                                             mk[0:64, n, :], ACT.Square)
            if n >= 1:
                h, s = n - 1, (n - 1) % 2
                bank = TB_ + s
                m = on(PE, squared[h], b, free[bank])(nc.tensor.matmul, ps[:96, bank, :TOK2], C("ones", rows)[:, :96],
                                                     B["ksq"][:, s, :], start=True, stop=True)
                r = inverse_rms(rn[rows, s, :], ps[:96, bank, :TOK2], 96, 1, m, last[s])
                free[bank] = r
                c = on(VE, r)(nc.vector.scalar_tensor_tensor, mk[0:64, h, :], mk[0:64, h, :], P2("g_k", slice(0, 64)),
                              rn[0:64, s, :], ALU.mult, ALU.mult)
                d = on(VE, r, roped)(nc.vector.tensor_tensor, mk[up, h, :], kr[up, :], rn[up, s, :], ALU.mult)
                last[s] = [m, c, d]
            yield
        ready += last[0] + last[1] + t_v

        def combine(E, f, a, m, L):
            return on(VE, a)(nc.vector.tensor_tensor, E, E, f.unsqueeze(2).to_broadcast([m, 2, L]), ALU.mult)

        def finish(g, a):
            B["o_done"].append(on(SC, a)(nc.scalar.activation, B["o"][:, g, :], ps[:, YB_, :TOK2], ACT.Copy))
            return B["o_done"][-1]

        yield from softmax_attention(
            B, range(4), lambda g, s: mq[:96, 2 * g + s, :], lambda g, s: mk[:96, 2 * g + s, :],
            lambda g, s, kt: mv[:TILES[kt][1], kt, 128 * g + 64 * s:128 * g + 64 * s + 64], 2, combine, finish, ready)

    def stick_breaking(B, toks):
        sq_, sk, sv, sp, ex, spm, exm = (B[n] for n in ("sbq", "sbk", "sbv", "sp", "ex", "spm", "exm"))
        read = []
        diag = lambda z: z.rearrange("p s (a b c) -> p s a b c", a=2, b=2)[:, :, :, 0, :]

        def apply(p, done):
            prog.wait(PE, done, free[YB_])
            for s in range(2):
                v = slice(128 * p + 64 * s, 128 * p + 64 * s + 64)
                y = ps[64 * s:64 * s + 64, YB_, :]
                nc.tensor.matmul(y[:, :TOK2], sv[:META, 2, v], exm[:, s, :], start=True, stop=True, skip_group_check=True)
                nc.tensor.matmul(y[:, META:TOK2], sv[:, 0, v], ex[:, s, :SEQ], start=False, stop=True, skip_group_check=True)
                m = nc.tensor.matmul(y[:, META + 128:TOK2], sv[:, 1, v], ex[:, s, SEQ:], start=False, stop=True,
                                     skip_group_check=True)
            m = prog.mark(PE, m)
            B["o_done"].append(on(SC, m, *B["o_read"])(nc.scalar.activation, B["o"][:, p, :], ps[:, YB_, :TOK2], ACT.Copy))
            free[YB_] = B["o_done"][-1]
            return m

        done = None
        for p in range(5):
            if p >= 1:
                read = [apply(p - 1, done)]
            if p == 4:
                break
            prog.wait(PE, free[SB_], free[TB_], free[TB_ + 1], *toks)
            for s in range(2):
                rows = slice(64 * s, 64 * s + 64)
                q, k = sq_[rows, p, :], sk[rows, p, :]
                nc.tensor.matmul(ps[:, SB_ + s, :SEQ], k[:, META:META + 128], q[:, META:], start=True, stop=True, skip_group_check=True)
                nc.tensor.matmul(ps[:, SB_ + s, SEQ:384], k[:, META + 128:], q[:, META + 128:], start=False, stop=True,
                                 skip_group_check=True)
                m = nc.tensor.matmul(ps[:META, TB_ + s, :TOK2], k[:, :META], q, start=True, stop=True, skip_group_check=True)
            m = prog.mark(PE, m)
            z, zm = ps[:, SB_:SB_ + 2, :384], ps[:META, TB_:TB_ + 2, :TOK2]
            prepared = []
            for src, t, dst in ((z, ex[:, :, :], sp[:, :, :384]), (zm, exm[:, :, :], spm[:, :, :])):
                a = on(SC, m, *read)(nc.scalar.activation, t, src, ACT.Abs)
                a = on(SC, a)(nc.scalar.activation, t, t, ACT.Exp, scale=-1.0)
                a = on(SC, a)(nc.scalar.activation, t, t, ACT.Ln, bias=C("ones", slice(0, t.shape[0]))[:, 0:1])
                prepared.append(on(VE, a)(nc.vector.scalar_tensor_tensor, dst, src, 0.0, t, ALU.max, ALU.add))
            one = C("strict_01").unsqueeze(1).unsqueeze(1).to_broadcast([128, 2, 2, 128])
            a = on(VE, prepared[0])(nc.vector.tensor_tensor, diag(sp), diag(sp), one, ALU.mult)
            last = spm[:, :, :META]
            b = on(VE, prepared[1])(nc.vector.tensor_tensor, last, last, C("strict_01", slice(0, META))[:, :META]
                                    .unsqueeze(1).to_broadcast([META, 2, META]), ALU.mult)
            yield
            prog.wait(PE, a, b)

            def add(dst, lhs, rhs):
                return nc.tensor.matmul(dst, lhs, rhs, start=False, stop=True, skip_group_check=True)

            for s in range(2):
                zs, s0, s1 = ps[:, SB_ + s, :], sp[:, s, :SEQ], sp[:, s, SEQ:384]
                add(zs[:, :SEQ], C("suffix"), s0)
                add(zs[:, 128:SEQ], C("minus"), s1)
                add(zs[:, :128], C("ident"), C("strict_neg"))
                add(zs[:, SEQ:384], C("suffix"), s1)
                m = add(zs[:, SEQ:384], C("ident"), C("strict_neg"))
            m0 = prog.mark(PE, m)
            for s in range(2):
                zs, s0, s1 = ps[:META, TB_ + s, :], sp[:, s, :SEQ], sp[:, s, SEQ:384]
                add(zs[:, :TOK2], C("suffix")[:META, :META], spm[:, s, :])
                add(zs[:, META:TOK2], C("minus")[:, :META], s0)
                add(zs[:, META + 128:TOK2], C("minus")[:, :META], s1)
                m = add(zs[:, :META], C("ident")[:META, :META], C("strict_neg")[:META, :META])
            m1 = prog.mark(PE, m)
            a = on(SC, m0)(nc.scalar.activation, ex[:, :, :], z, ACT.Exp)
            b = on(SC, m1)(nc.scalar.activation, exm[:, :, :], zm, ACT.Exp)
            free[SB_], free[TB_], free[TB_ + 1] = a, b, b
            done = [a, b]
            yield

    def differential(B, heads, t_v):
        dq, dk, dv, rn = B["dq"], B["dk"], B["dv"], B["rn"]
        rows = slice(0, 128)
        names = ("rot_diff", "cos_diff", "sin_diff")
        todo = [(z[:, h, :], rows, P2(g), "blk64", names, 64, f, heads[n])
                for z, g, f, n in ((dq, "g_dq", 64, "q"), (dk, "g_dk", 1, "k")) for h in range(4)]
        for done in rope_norms(todo, B):
            yield
        ready = done[-2:] + t_v
        B["rn_read"] = done[-2:]

        def combine(E, f, a, m, L):
            a = on(VE, a)(nc.vector.tensor_tensor, f[:, 1:2], f[:, 1:2], B["neg_lam"][:m, :], ALU.mult)
            a = on(VE, a)(nc.vector.tensor_scalar, E[:, 1, :], E[:, 1, :], f[:, 1:2], None, ALU.mult)
            return on(VE, a)(nc.vector.scalar_tensor_tensor, E[:, 0, :], E[:, 0, :], f[:, 0:1], E[:, 1, :], ALU.mult, ALU.add)

        pending, sq_read = [], [None, None]

        def normalise():
            h, t = pending.pop(0)
            m = on(PE, t, free[TB_])(nc.tensor.matmul, ps[:, TB_, :TOK2], C("ones"), sq[:, h % 2, :TOK2], start=True, stop=True)
            sq_read[h % 2] = m
            r = inverse_rms(rn[:, 0, :], ps[:, TB_, :TOK2], 128, 1, m, *B["rn_read"])
            free[TB_] = r
            a = on(VE, r, t)(nc.vector.scalar_tensor_tensor, B["o"][:, h, :], B["o"][:, h, :], B["g_out"][:, :],
                             rn[:, 0, :], ALU.mult, ALU.mult)
            B["rn_read"] = [a]
            B["o_done"].append(a)

        def finish(h, a):
            c = on(SC, a, *B["o_read"])(nc.scalar.activation, B["o"][:, h, :], ps[:, YB_, :TOK2], ACT.Copy)
            t = on(SC, c, sq_read[h % 2])(nc.scalar.activation, sq[:, h % 2, :TOK2], ps[:, YB_, :TOK2], ACT.Square)
            pending.append((h, t))
            return t

        steps = softmax_attention(
            B, range(4), lambda g, s: dq[64 * s:64 * s + 64, g, :], lambda g, s: dk[64 * s:64 * s + 64, g, :],
            lambda g, s, kt: dv[:TILES[kt][1], kt, 128 * g:128 * g + 128], 1, combine, finish, ready)
        for _ in steps:
            yield
            if pending:
                normalise()
        while pending:
            normalise()

    def second_layer(i):
        nt = TOK2
        stream.start_layer(i + DEPTH, COLS2)
        nc.scalar.dma_start(params[:, :n_par2], ins["params2"][bass.ds(i, 1)].rearrange("a p n -> (a p) n"))\
            .then_inc(loaded, 16)
        for e in (SC, VE, PE):
            prog.engines[e].wait_ge(loaded, 16)
        his, lows = rmsnorm(nt, P2("g_ln1"), [], [])
        act = (h_hi, h_lo)

        def track(evacuate, into):
            def wrapped(c, b, t):
                tok = evacuate(c, b, t)
                into.append(tok)
                return tok
            return wrapped

        with ExitStack() as own:
            def buf(name, *shape, dt=F32, into=own.enter_context, parts=128):
                return sbuf("b2_" + name, parts, *shape, dt=dt, into=into)

            B = {"mv": buf("mv", 3, 512), "sbv": buf("sbv", 3, 512), "dv": buf("dv", 3, 512),
                 "sbq": buf("sbq", 4, nt), "sbk": buf("sbk", 4, nt), "dq": buf("dq", 4, nt), "dk": buf("dk", 4, nt),
                 "o": buf("o", 4, nt), "rn": buf("rn", 2, nt), "rot": buf("rot", 2, nt), "kr": buf("kr", nt),
                 "small": buf("small", 2, 3, 2), "neg_lam": buf("neg_lam", 1), "g_out": buf("g_out", 1),
                 "lam": buf("lam_sums", 2), "o_done": [], "o_read": []}
            o_hi, o_lo = (buf(f"o_{n}", 4, nt, dt=F32R) for n in ("hi", "lo"))
            gate = buf("gate", KC, nt)
            shared = ExitStack()
            B["mq"], B["mk"] = (buf(n, 8, nt, into=shared.enter_context) for n in ("mq", "mk"))
            inner = ExitStack()
            c32 = buf("c32", 3, nt, into=inner.enter_context)
            c_hi, c_lo = (buf(f"c_{n}", 3, nt, dt=F32R, into=inner.enter_context) for n in ("hi", "lo"))
            lam = P2("lam").rearrange("p (a b) -> p a b", b=2)
            a = on(VE)(nc.vector.tensor_tensor, B["lam"][:, :], lam[:, :, 0], lam[:, :, 1], ALU.mult)
            m = on(PE, a, free[TB_ + 1])(nc.tensor.matmul, ps[:, TB_ + 1, 0:2], C("ones"), B["lam"][:, :], start=True, stop=True)
            a = on(SC, m)(nc.scalar.activation, B["lam"][:, :], ps[:, TB_ + 1, 0:2], ACT.Exp)
            free[TB_ + 1] = a
            a = on(VE, a)(nc.vector.tensor_tensor, B["neg_lam"][:, :], B["lam"][:, 1:2], B["lam"][:, 0:1], ALU.subtract)
            t_lam = on(VE, a)(nc.vector.tensor_tensor, B["neg_lam"][:, :], B["neg_lam"][:, :], P2("lam_init"), ALU.subtract)
            t_lam = on(VE, t_lam)(nc.vector.tensor_tensor, B["g_out"][:, :], P2("g_do"), P2("one_less"), ALU.mult)
            t_c, t_kr = [], []
            project(0, KC, act, nt, track(copy_to(lambda c: c32[:, c, :]), t_c), his, lows)

            def latents(c, b, t):
                if c == 0:
                    t_c.append(on(SC, t)(nc.scalar.activation, c32[:, 2, :], ps[:, b, :nt], ACT.Copy))
                    return t_c[-1]
                t_kr.append(on(SC, t)(nc.scalar.activation, B["kr"][64:96, :], ps[64:96, b, :nt], ACT.Copy))
                return t_kr[-1]
            project(1, KC, act, nt, latents)
            t_latent = []

            def norm_latents():
                prev = None
                for first, n, gain in ((0, 2, "g_cq"), (2, 1, "g_ckv")):
                    sqs = [on(SC, *t_c, prev)(nc.scalar.activation, sq[:, k, :nt], c32[:, first + k, :], ACT.Square)
                           for k in range(n)]
                    yield
                    prog.wait(PE, free[TB_], *sqs)
                    for k in range(n):
                        m = nc.tensor.matmul(ps[:, TB_, :nt], C("ones"), sq[:, k, :nt], start=k == 0, stop=k == n - 1)
                    prev = m = prog.mark(PE, m)
                    rd = t_latent[-1] if t_latent else None
                    r = inverse_rms(B["rn"][:, 0, :], ps[:, TB_, :nt], 128 * n, 1, m, rd)
                    free[TB_] = r
                    for k in range(n):
                        v = c32[:, first + k, :]
                        a = on(VE, r)(nc.vector.scalar_tensor_tensor, v, v, P2(gain)[:, k:k + 1], B["rn"][:, 0, :], ALU.mult, ALU.mult)
                        t_latent.append(a)
                        split_done.append(split(v, c_hi[:, first + k, :], c_lo[:, first + k, :], a))
                    yield
            split_done = []
            state["filler"] = norm_latents()
            t_sb = []

            def scaled(n):
                def evacuate(c, b, t):
                    return on(SC, t)(nc.scalar.activation, B["sbq"][:, 2 * n + c, :], ps[:, b, :nt], ACT.Copy, scale=0.125)
                return evacuate
            for n in range(2):
                project(2 + n, KC, act, nt, track(scaled(n), t_sb))
            for n in range(2):
                project(4 + n, KC, act, nt, track(copy_to(lambda c, n=n: B["sbk"][:, 2 * n + c, :]), t_sb))
            finish_filler()
            heads = {"q": [], "k": [], "kr": t_kr}
            hs, ls = zip(*split_done)
            project(6, 2, (c_hi, c_lo), nt, track(copy_to(lambda c: B["mq"][:96, c, :]), heads["q"]), hs[:2], ls[:2])
            w = stream.view(7, 1)
            for t_ in range(8):
                b = next_bank()
                prog.wait(PE, free[b])
                cols = slice(128 * t_, 128 * t_ + 128)
                t = stream.product(7, ps[:, b, :nt], [((w[0][:, 0, cols], w[1][:, 0, cols]),
                                                       (c_hi[:, 2, :], c_lo[:, 2, :]), True)], late=[ls[2]], lows=[hs[2]])
                heads["k"].append(on(SC, t)(nc.scalar.activation, B["mk"][0:64, t_, :], ps[0:64, b, :nt], ACT.Copy))
                free[b] = heads["k"][-1]
            t_v = []
            w = [z.rearrange("p k (h two d) -> p k h two d", h=8, two=2)[:, 0, :, 1, :] for z in w]
            for n, (a0, m) in enumerate(TILES):
                b = next_bank()
                prog.wait(PE, free[b])
                lhs = [z[:, 2, a0:a0 + 128] for z in (c_hi, c_lo)]
                t = stream.product(7, ps[:, b, :], [(lhs, w, False)])
                if n == 0:
                    stream.split_next()
                t_v.append(on(SC, t)(nc.scalar.activation, B["mv"][:m, n, :], ps[:m, b, :], ACT.Copy))
                free[b] = t_v[-1]
            inner.close()
            work = ExitStack()
            top = work.enter_context
            B["ksq"] = buf("ksq", 2, nt, into=top, parts=96)
            B["e"], B["pt"] = buf("e", 2, 2, nt, into=top), buf("pt", 512, into=top)
            B["ptm"] = buf("ptm", 256, into=top, parts=META)
            for e in (SC, VE, PO):
                prog.wait(e, prog.now(PE, SC, VE, PO))
            B["e"], B["pt"], B["ptm"] = B["e"][:, :, :, :], B["pt"][:, :], B["ptm"][:, :]
            state["filler"] = mla(B, heads, t_v)
            t_sv, t_d, t_dv = [], {"q": [], "k": []}, []

            def values(u, dst, into):
                for n in range(2):
                    def evacuate(c, b, t, n=n):
                        m = TILES[c][1]
                        return on(SC, t)(nc.scalar.activation, dst[:m, c, 256 * n:256 * n + 256], ps[:m, b, :256], ACT.Copy)
                    project_tokens(u + n, KC, act, TILES, 256, track(evacuate, into))

            values(8, B["sbv"], t_sv)
            for n in range(2):
                project(10 + n, KC, act, nt, track(copy_to(lambda c, n=n: B["dq"][:, 2 * n + c, :]), t_d["q"]))
            for n in range(2):
                project(12 + n, KC, act, nt, track(copy_to(lambda c, n=n: B["dk"][:, 2 * n + c, :]), t_d["k"]))
            values(14, B["dv"], t_dv)
            u, merged_done, branch_read = 16, [], []
            t_gate = []
            for branch in range(3):
                t_gate = []
                for n in range(4):
                    def evacuate(c, b, t, n=n):
                        k = 2 * n + c
                        return on(SC, t, *branch_read)(nc.scalar.activation, gate[:, k, :], ps[:, b, :nt], ACT.Identity,
                                                       bias=P2("gate_b")[:, KC * branch + k:KC * branch + k + 1])
                    project(u + n, KC, act, nt, track(evacuate, t_gate))
                u += 4
                finish_filler()
                if branch == 0:
                    work.close()
                    shared.close()
                    merged = buf("merged", KC, nt)
                    B["ex"], B["sp"] = buf("ex", 2, 384), buf("sp", 2, 512)
                    B["exm"], B["spm"] = (buf(n, 2, nt, parts=META) for n in ("exm", "spm"))
                    B["e"], B["pt"] = buf("e2", 2, 2, nt)[:, :, :, :], buf("pt2", 512)[:, :]
                    B["ptm"] = buf("ptm2", 256, parts=META)[:, :]
                    for e in (SC, VE, PO):
                        prog.wait(e, prog.now(PE, SC, VE, PO))
                g = gate[:, :, :].rearrange("p k t -> p (k t)")
                t_sig = on(SC, *t_gate)(nc.scalar.activation, g, g, ACT.Sigmoid)
                nc.scalar.preload_act_table_set("natural_log_exp_and_others")
                o_hs, o_ls = [], []
                for k in range(4):
                    th, tl = split(B["o"][:, k, :], o_hi[:, k, :], o_lo[:, k, :], *B["o_done"], *branch_read)
                    o_hs.append(th)
                    o_ls.append(tl)
                B["o_read"], B["o_done"] = o_hs + o_ls, []
                if branch == 0:
                    state["filler"] = stick_breaking(B, t_sb + t_sv)
                elif branch == 1:
                    prog.wait(VE, t_lam)
                    state["filler"] = differential(B, t_d, t_dv)

                def merge(n, branch=branch, t_sig=t_sig):
                    def evacuate(c, b, t):
                        k = 4 * n + c
                        if branch == 0:
                            a = on(VE, t, t_sig)(nc.vector.tensor_tensor, merged[:, k, :], gate[:, k, :], ps[:, b, :nt], ALU.mult)
                            merged_done.append(a)
                            branch_read.append(a)
                            return a
                        a = on(VE, t, t_sig)(nc.vector.tensor_tensor, gate[:, k, :], gate[:, k, :], ps[:, b, :nt], ALU.mult)
                        c = on(PO, a, merged_done[k])(nc.gpsimd.tensor_tensor, merged[:, k, :], merged[:, k, :], gate[:, k, :], ALU.add)
                        merged_done[k] = c
                        branch_read.append(c)
                        return a
                    return evacuate

                branch_read.clear()
                for n in range(2):
                    project(u + n, 4, (o_hi, o_lo), nt, merge(n), o_hs, o_ls)
                u += 2
                branch_read += prog.now(PE)
            h_read = prog.now(PE)
            his, lows = [], []
            for k in range(KC):
                th, tl = split(merged[:, k, :], h_hi[:, k, :], h_lo[:, k, :], merged_done[k], *h_read,
                               low_on=VE if k % 2 else PO)
                his.append(th)
                lows.append(tl)
            x_done = []
            for n in range(4):
                project(u + n, KC, act, nt, add_to_residual(nt, 2 * n, x_done), his, lows)
            u += 4
        his, lows = rmsnorm(nt, P2("g_ln2"), x_done, prog.now(PE))
        u, x_done = mlp(u, nt, his, lows, None, "b2")
        assert u == UNITS - 2

    rounds = [PE, SC, VE, PO]
    kinds = [prog.engines[e].engine for e in rounds]
    counts = [prog.sems[e] for e in rounds] + [loaded]
    numbers = range(counts[0].num, counts[-1].num + 1)

    def next_round():
        nc.multi_engine_barrier(kinds, sems_to_clear=numbers)
        prog.restart()
        for b in free:
            free[b] = None

    stream.load_all(ins["stream"])
    nc.scalar.dma_start(consts[:, :own0], ins["consts"][:, :own0]).then_inc(loaded, 16)
    nc.scalar.dma_start(consts[:, own0:own0 + n1], ins["consts"][:, own0:own0 + n1]).then_inc(loaded, 16)
    nc.scalar.dma_start(x[:, :, META:], ins["x"]).then_inc(loaded, 16)
    nc.scalar.dma_start(x[:, :, :META], ins["meta"]).then_inc(loaded, 16)
    for e in rounds:
        prog.engines[e].wait_ge(loaded, 64)
    next_round()
    with nc.Fori(0, DEPTH, engines=kinds) as i:
        nc.scalar.preload_act_table_set("natural_log_exp_and_others")
        first_layer(i)
        next_round()
    if LAYERS > DEPTH:
        nc.scalar.dma_start(consts[:, own0:own0 + n2], ins["consts"][:, own0 + n1:]).then_inc(loaded, 16)
        for e in rounds:
            prog.engines[e].wait_ge(loaded, 16)
        next_round()
        with nc.Fori(0, DEPTH, engines=kinds) as i:
            nc.scalar.preload_act_table_set("natural_log_exp_and_others")
            second_layer(i)
            next_round()
    nc.scalar.dma_start(out, x[:, :, META:]).then_inc(stored, 16)
    nc.scalar.wait_ge(stored, 16)


def _chunks(w, kcs):
    n = w.shape[1]
    u = np.ascontiguousarray(w.reshape(kcs, 128, n).transpose(1, 0, 2)).reshape(128, kcs * n)
    return np.pad(u, ((0, 0), (0, UNIT - u.shape[1]))) if u.shape[1] < UNIT else u


def _units(w, kcs, cols):
    return [_chunks(w[:, a:a + cols], kcs) for a in range(0, w.shape[1], cols)]


def _first_units(a, i):
    w = a["w_in"][i]
    at = np.cumsum([0, 512, 128, 128, 128, 128, 128, 128, 24, 512, 512, 512, 512, 1024, 1024])
    q, kc, vc, ks, vs, kw, vw, gate, rq, rk, rv, rg, ma, mb = (w[:, at[n]:at[n + 1]] for n in range(14))
    twice = lambda z: z.reshape(D, 2, 1, 64).repeat(2, axis=2).reshape(D, 256)
    heads = lambda z: z.reshape(-1, 2, 4, 64).transpose(0, 2, 1, 3).reshape(-1, 512)
    units = [_chunks(twice(kc), KC), _chunks(twice(vc), KC)] + _units(heads(q), KC, 256)
    units += [_chunks(np.concatenate([ks, kw], 1), KC), _chunks(np.concatenate([vs, vw], 1), KC), _chunks(gate, KC)]
    for n in ("cmp_w1_k", "cmp_w1_v"):
        units += _units(a[n][i], 16, 128)
    for z in (rq, rk, rv, rg, ma, mb):
        units += _units(z, KC, 256)
    up = a["w_up_nsa"][i].reshape(2, 4, 64, D).transpose(1, 0, 2, 3).reshape(512, D)
    units += _units(up, 4, 512) + _units(a["w_up_ret"][i], 4, 512) + _units(a["w_out"][i], KC, 256)
    units += _units(a["w_ff1"][i], KC, 256)
    for c in range(0, D, 256):
        units += [_chunks(a["w_ff2"][i][r:r + D, c:c + 256], KC) for r in range(0, FF, D)]
    units += _units(a["w_ple"][i], 2, D) + _units(a["w_ple_gate"][i], KC, 256)
    return units


def _columns(v):
    return v.reshape(-1, 128).T


def _first_params(a, i):
    twice = lambda v: np.concatenate([v, v])[:, None]
    rows = lambda z: z.reshape(16, 2, 64).transpose(1, 2, 0).reshape(128, 16)
    w2 = lambda z: z.reshape(2, 128, 64).transpose(1, 0, 2).reshape(128, 128)
    p = a["p"][i, 0].T.reshape(2, 128, SEQ).transpose(1, 0, 2).reshape(128, 2 * SEQ)
    return np.concatenate([_columns(a["norm_mix"][i]), _columns(a["norm_mlp"][i]), _columns(a["norm_ple"][i]),
                           twice(a["nsa_q_norm"][i]), twice(a["nsa_k_norm"][i]), rows(a["cmp_pos_k"][i]),
                           rows(a["cmp_pos_v"][i]), w2(a["cmp_w2_k"][i]), w2(a["cmp_w2_v"][i]), p], axis=1)


def _second_units(a, i):
    w = a["w_in_2"][i]
    at = np.cumsum([0, 256, 128, 32, 512, 512, 512, 512, 512, 512, 3 * D])
    cq, ckv, kr, sq, sk, sv, dq, dk, dv, gates = (w[:, at[n]:at[n + 1]] for n in range(10))
    units = [_chunks(cq, KC), _chunks(np.concatenate([ckv, np.pad(kr, ((0, 0), (64, 32)))], 1), KC)]
    for z in (sq, sk):
        units += _units(z, KC, 256)
    uq = np.pad(a["mla_w_uq_2"][i].reshape(256, 8, 96), ((0, 0), (0, 0), (0, 32))).reshape(256, 1024)
    units += [_chunks(uq, 2), _chunks(a["mla_w_ukv_2"][i], 1)]
    for z in (sv, dq, dk, dv):
        units += _units(z, KC, 256)
    for n in range(3):
        units += _units(gates[:, n * D:n * D + D], KC, 256)
        units += _units(a["w_branch_2"][i][512 * n:512 * n + 512], 4, 512)
    units += _units(a["w_out_2"][i], KC, 256) + _units(a["w_ff1_2"][i], KC, 256)
    for c in range(0, D, 256):
        units += [_chunks(a["w_ff2_2"][i][r:r + D, c:c + 256], KC) for r in range(0, FF, D)]
    return units + [np.zeros((128, UNIT), np.float32)] * 2


def _second_params(a, i):
    def rows(v, *at):
        out = np.zeros((128, 1), np.float32)
        for b in at:
            out[b:b + len(v), 0] = v
        return out

    lam = np.zeros((128, 4), np.float32)
    lam[:64] = a["diff_lambda_2"][i].T
    lam_init = 0.8 - 0.6 * np.exp(-0.3 * i)
    full = lambda v: np.full((128, 1), v, np.float32)
    return np.concatenate([_columns(a["ln1_g_2"][i]), _columns(a["ln2_g_2"][i]), _columns(a["mla_cq_norm_g_2"][i]),
                           _columns(a["mla_ckv_norm_g_2"][i]), rows(a["mla_q_norm_g_2"][i], 0),
                           rows(a["mla_k_norm_g_2"][i], 0), rows(a["diff_q_norm_g_2"][i], 0, 64),
                           rows(a["diff_k_norm_g_2"][i], 0, 64), _columns(a["diff_out_norm_g_2"][i]), lam,
                           full(lam_init), full(1.0 - lam_init), _columns(a["gate_b_2"][i])], axis=1)


def host_arrays(inputs):
    a = {k: np.asarray(v) for k, v in inputs.items()}
    units = []
    for i in range(DEPTH):
        units += _first_units(a, i)
    if LAYERS > DEPTH:
        for i in range(DEPTH):
            units += _second_units(a, i)
    arrays = {"stream": np.stack(units), "consts": np.concatenate(list(const_tables().values()), axis=1),
              "x": a["x"][0].T.reshape(KC, 128, SEQ).transpose(1, 0, 2),
              "meta": a["meta_tokens_2"].T.reshape(KC, 128, META).transpose(1, 0, 2),
              "params1": np.stack([_first_params(a, i) for i in range(DEPTH)])}
    if LAYERS > DEPTH:
        arrays["params2"] = np.stack([_second_params(a, i) for i in range(DEPTH)])
    assert arrays["stream"].shape == (LAYERS * UNITS, 128, UNIT)
    return {k: np.ascontiguousarray(v) for k, v in arrays.items()}


def kernel(**inputs):
    import concourse.bacc as bacc
    from concourse.bass_utils import run_bass_kernel_spmd

    nc = bacc.Bacc("TRN2", target_bir_lowering=False, num_devices=1)
    arrays, aps = {}, {}
    for name, v in host_arrays(inputs).items():
        arrays[f"in_{name}"] = v
        aps[name] = nc.dram_tensor(f"in_{name}", v.shape, mybir.dt.from_np(v.dtype), kind="ExternalInput").ap()
    out = nc.dram_tensor("out_x", (128, KC, SEQ), F32, kind="ExternalOutput").ap()
    build(nc, aps, out)
    r = run_bass_kernel_spmd(nc, [arrays], core_ids=[0])
    y = np.asarray(r.results[0]["out_x"]).reshape(128, KC, SEQ)
    return np.ascontiguousarray(y.transpose(2, 1, 0)).reshape(1, SEQ, D)
```

```python
from contextlib import ExitStack

import numpy as np
import concourse.bass as bass
from concourse import mybir

ALU = mybir.AluOpType
ACT = mybir.ActivationFunctionType
F32 = mybir.dt.float32
F32R = mybir.dt.float32r
BF16 = mybir.dt.bfloat16
AX = mybir.AxisListType.X

D, DEPTH, SEQ, META = 1024, 2, 256, 16
KC = D // 128
TOK2 = SEQ + META
FF = 4 * D
EPS = 1e-6
NEG = -1e30

UNIT = 2048
NRAW, NSPL = 3, 3
AHEAD = NSPL - 1
UNITS = 72
LAYERS = 2 * DEPTH
TO_DVE = 1152

GB = (0, 1, 2)
SB_, TB_, YB_ = 3, 5, 7

PE, SC, VE, PO = "tensor", "scalar", "vector", "gpsimd"


def const_tables():
    c = {}
    i = np.arange(128)
    c["ident"] = np.eye(128)
    c["ones"] = np.ones((128, 128))
    c["blk64"] = (i[:, None] // 64 == i[None, :] // 64) * 1.0
    c["causal_neg"] = np.where(i[None, :] <= i[:, None], 0.0, NEG)
    c["strict_neg"] = np.where(i[:, None] < i[None, :], 0.0, NEG)
    c["strict_01"] = (i[:, None] < i[None, :]) * 1.0
    c["suffix"] = np.where(i[:, None] >= i[None, :], -1.0, 0.0)
    c["minus"] = -np.ones((128, 128))

    def rotation(size, half, first):
        r = np.zeros((128, 128))
        for base in range(first, size, 2 * half):
            for a in range(half):
                r[base + half + a, base + a] = -1.0
                r[base + a, base + half + a] = 1.0
        return r

    c["rot_ret"] = rotation(128, 64, 0)
    c["rot_diff"] = rotation(128, 32, 0)
    c["rot_mla"] = rotation(96, 16, 64)
    f32 = np.float32
    inv = f32(10000.0) ** (-np.arange(64, dtype=f32) / f32(64))
    ang = (np.arange(SEQ, dtype=f32)[:, None] * inv[None, :]).astype(f32)
    c["cos_ret"] = np.tile(np.cos(ang).T, (2, 1))
    c["sin_ret"] = np.tile(np.sin(ang).T, (2, 1))
    pos = np.arange(TOK2, dtype=f32)

    def angles(d):
        inv = np.exp(f32(-np.log(10000.0)) * (f32(2.0) * np.arange(d // 2, dtype=f32) / f32(d)))
        return (pos[:, None] * inv[None, :].astype(f32)).astype(f32)

    a = angles(64)
    c["cos_diff"] = np.tile(np.cos(a).T, (4, 1))
    c["sin_diff"] = np.tile(np.sin(a).T, (4, 1))
    a = angles(32)
    cm, sm = np.ones((128, TOK2)), np.zeros((128, TOK2))
    cm[64:96] = np.tile(np.cos(a).T, (2, 1))
    sm[64:96] = np.tile(np.sin(a).T, (2, 1))
    c["cos_mla"], c["sin_mla"] = cm, sm
    dec = []
    for h in range(4):
        lg = np.log(1.0 - 2.0 ** (-5.0 - h))
        n = np.arange(SEQ)
        diff = n[None, :] - i[:, None]
        first = np.where(diff >= 0, np.exp(lg * np.maximum(diff, 0)), 0.0) * 128 ** -0.5
        dec.append(np.concatenate([first, first[:, :128]], axis=1))
    c["decay"] = np.concatenate(dec, axis=1)
    q = np.arange(SEQ).reshape(2, 128).T
    ok = (16 * np.arange(16) + 31)[None, None, :] <= q[:, :, None]
    c["cmp_neg"] = np.where(ok, 0.0, NEG).reshape(128, 32)
    c["cmp_01"] = (ok * 1.0).reshape(128, 32)
    c["eps"] = np.full((128, 1), EPS)
    c["eps64"], c["eps96"] = np.full((128, 1), 64 * EPS), np.full((128, 1), 96 * EPS)
    order = [*BOTH, *FIRST, *(k for k in c if k not in BOTH + FIRST)]
    return {k: np.ascontiguousarray(c[k], dtype=np.float32) for k in order}


def offsets(sizes):
    at, out = 0, {}
    for name, n in sizes:
        out[name] = (at, n)
        at += n
    return out, at


BOTH = ("ident", "ones", "blk64", "causal_neg", "eps", "eps64", "eps96")
FIRST = ("rot_ret", "cos_ret", "sin_ret", "decay", "cmp_neg", "cmp_01")


def const_places(tables):
    sizes = lambda names: [(k, tables[k].shape[1]) for k in names]
    both, own = offsets(sizes(BOTH))
    first, n1 = offsets(sizes(FIRST))
    second, n2 = offsets(sizes([k for k in tables if k not in BOTH + FIRST]))
    at = dict(both)
    at.update({k: (own + a, n) for k, (a, n) in {**first, **second}.items()})
    return at, own, n1, n2


PARAMS1 = [("g_mlp", 8), ("g_ple", 8), ("g_next", 8), ("g_q", 1), ("g_k", 1), ("pos_k", 16), ("pos_v", 16),
           ("w2_k", 128), ("w2_v", 128), ("p", 2 * SEQ)]
PARAMS2 = [("g_ln2", 8), ("g_next", 8), ("g_cq", 2), ("g_ckv", 1), ("g_q", 1), ("g_k", 1), ("g_dq", 1),
           ("g_dk", 1), ("g_do", 1), ("lam", 4), ("lam_init", 1), ("one_less", 1), ("gate_b", 24)]


class Progress:

    def __init__(self, nc, sems):
        self.engines = {PE: nc.tensor, SC: nc.scalar, VE: nc.vector, PO: nc.gpsimd}
        self.sems = sems
        self.restart()

    def restart(self):
        self.count = {e: 0 for e in self.engines}
        self.seen = {}

    def wait(self, engine, *tokens):
        for t in tokens:
            if isinstance(t, list):
                self.wait(engine, *t)
            elif t is not None and self.seen.get((engine, t[0]), 0) < t[1]:
                self.engines[engine].wait_ge(self.sems[t[0]], t[1])
                self.seen[engine, t[0]] = t[1]

    def mark(self, engine, instruction):
        self.count[engine] += 1
        instruction.then_inc(self.sems[engine], 1)
        return (engine, self.count[engine])

    def on(self, engine, *tokens):
        self.wait(engine, *tokens)
        return lambda build, *a, **k: self.mark(engine, build(*a, **k))

    def now(self, *engines):
        return [(e, self.count[e]) for e in engines if self.count[e]]


class Stream:

    def __init__(self, nc, prog, enter):
        self.nc, self.prog = nc, prog
        self.raw = enter(nc.sbuf_tensor("raw_units", [128, NRAW, UNIT], F32))
        self.hi = enter(nc.sbuf_tensor("units_hi", [128, NSPL, UNIT], F32R))
        self.lo = enter(nc.sbuf_tensor("units_lo", [128, NSPL, UNIT], F32R))
        self.landed = [enter(nc.semaphore(f"landed_{s}")) for s in range(NRAW)]
        self.hi_made = [enter(nc.semaphore(f"hi_made_{s}")) for s in range(NSPL)]
        self.lo_made = {e: [enter(nc.semaphore(f"lo_made_{e}_{s}")) for s in range(NSPL)] for e in (VE, PO)}

    def load_all(self, stream, afterwards):
        sp, body = self.nc.sync, NRAW * NSPL

        def load(i, n):
            back = n - NRAW
            if not (isinstance(i, int) and i == 0 and back < 0):
                turn = (i * (body // NSPL) + (back // NSPL + 1)) * 2
                for e in (VE, PO):
                    sp.wait_ge(self.lo_made[e][back % NSPL], turn)
            src = stream[bass.ds(n if isinstance(i, int) else i * body + n, 1)].rearrange("a p n -> (a p) n")
            sp.dma_start(self.raw[:, n % NRAW, :], src).then_inc(self.landed[n % NRAW], 16)

        for n in range(body):
            load(0, n)
            if n == NRAW - 1:
                afterwards()
        with sp.Fori(1, LAYERS * UNITS // body) as i:
            for n in range(body):
                load(i, n)
        for n in range(AHEAD):
            load(LAYERS * UNITS // body, n)

    def start_layer(self, layer, columns):
        self.layer, self.columns = layer, columns + [UNIT] * AHEAD
        self.used, self.next, self.seen = {}, AHEAD, {}

    def split_first(self):
        self.layer, self.columns, self.used, self.next = 0, [UNIT] * AHEAD, {}, 0
        for _ in range(AHEAD):
            self.split_next(0)()
            self.split_next(1)()

    def split_next(self, half):
        u = self.next
        self.next += half
        nc, prog, r, s, n = self.nc, self.prog, u % NRAW, u % NSPL, self.columns[u]
        begin, end = half * (n // 2), (half + 1) * (n // 2)
        freed = self.used.get(u - NSPL)
        turn = self.layer * (UNITS // NSPL) * 2 + (u // NSPL * 2 + half + 1)
        prog.wait(SC, freed)
        nc.scalar.wait_ge(self.landed[r], (self.layer * (UNITS // NRAW) + (u // NRAW + 1)) * 16)
        nc.scalar.activation(self.hi[:, s, begin:end], self.raw[:, r, begin:end], ACT.Copy).then_inc(self.hi_made[s], 1)
        cut = begin + (end - begin) * TO_DVE // UNIT // 2 * 2

        def lower():
            for e, a, b in ((VE, begin, cut), (PO, cut, end)):
                eng = prog.engines[e]
                prog.wait(e, freed)
                eng.wait_ge(self.hi_made[s], turn)
                eng.tensor_tensor(self.lo[:, s, a:b], self.raw[:, r, a:b], self.hi[:, s, a:b].bitcast(F32),
                                  ALU.subtract).then_inc(self.lo_made[e][s], 1)
        return lower

    def need(self, u, part):
        if self.seen.get((u, part)):
            return
        self.seen[u, part] = True
        turn = (self.layer * (UNITS // NSPL) + (u // NSPL + 1)) * 2
        sems = [self.hi_made[u % NSPL]] if part == "hi" else [self.lo_made[e][u % NSPL] for e in (VE, PO)]
        for sem in sems:
            self.nc.tensor.wait_ge(sem, turn)

    def view(self, u, kcs):
        n = self.columns[u]
        return [t[:, u % NSPL, :n].rearrange("p (k c) -> p k c", k=kcs) for t in (self.hi, self.lo)]

    def product(self, u, out, pairs, start=True, stop=True, his=(), lows=(), tail=0):
        nc, prog = self.nc, self.prog
        n, todo = len(pairs), []
        for ks in (range(n - tail), range(n - tail, n)):
            todo += [(part, k) for part in range(3) for k in ks]
        for at, (part, k) in enumerate(todo):
            a, b, w_first = pairs[k]
            wl, xl = int(part == 1), int(part == 2)
            self.need(u, "lo" if part == 1 else "hi")
            if part == 2 and lows:
                prog.wait(PE, lows[k])
            elif his:
                prog.wait(PE, his[k])
            a, b = (a[wl], b[xl]) if w_first else (a[xl], b[wl])
            m = nc.tensor.matmul(out, a, b, start=start and at == 0, stop=stop and at == len(todo) - 1,
                                 skip_group_check=True)
        t = prog.mark(PE, m)
        self.used[u] = t
        return t


def build(nc, ins, out):
    with ExitStack() as ctx:
        _build(nc, ins, out, ctx.enter_context)


def _build(nc, ins, out, enter):
    tables = const_tables()
    at_const, own0, n1, n2 = const_places(tables)
    n_const = own0 + max(n1, n2)
    at_par1, n_par1 = offsets(PARAMS1)
    at_par2, n_par2 = offsets(PARAMS2)

    prog = Progress(nc, {e: enter(nc.semaphore(f"done_{e}")) for e in (PE, SC, VE, PO)})
    on = prog.on
    loaded = enter(nc.semaphore("loaded"))
    both_in = enter(nc.semaphore("both_in"))
    consts_in = enter(nc.semaphore("consts_in"))
    stream = Stream(nc, prog, enter)
    stored = enter(nc.semaphore("stored"))

    def sbuf(name, *shape, dt=F32, into=enter):
        return into(nc.sbuf_tensor(name, list(shape), dt))

    ps = enter(nc.psum_tensor("ps", [128, 8, 512], F32))
    consts = sbuf("consts", 128, n_const)
    x = sbuf("x_res", 128, KC, TOK2)
    h_hi, h_lo = (sbuf(f"h_{n}", 128, KC, TOK2, dt=F32R) for n in ("hi", "lo"))
    sq = sbuf("sq", 128, 2, 512)
    tmp = sbuf("tmp", 128, 2, TOK2)
    sums = sbuf("sums", 128, TOK2)
    rs = sbuf("rs", 128, TOK2 + 3)
    neg_rs = sbuf("neg_rs", 128, 2)
    ident_b, causal_b, strict_b = (sbuf(n, 128, 128, dt=BF16) for n in ("ident_b", "causal_b", "strict_b"))
    start_gains = sbuf("start_gains", 128, 2 * KC)
    params = sbuf("params", 128, max(n_par1, n_par2))

    def C(name, parts=slice(0, 128)):
        a, n = at_const[name]
        return consts[parts, a:a + n]

    def P1(name):
        a, n = at_par1[name]
        return params[:, a:a + n]

    def P2(name, parts=slice(0, 128)):
        a, n = at_par2[name]
        return params[parts, a:a + n]

    free = {b: None for b in range(8)}
    state = {"bank": 0, "filler": None}

    def next_bank():
        b = GB[state["bank"] % len(GB)]
        state["bank"] += 1
        return b

    later = []

    def flush():
        while later:
            later.pop(0)()

    def leave(evacuate, c, b, t, halves=()):
        before, later[:] = later[:], []
        free[b] = evacuate(c, b, t)
        for put_off in before:
            put_off()
        for half in halves:
            later.append(stream.split_next(half))

    def fill(n=1):
        for _ in range(n):
            if state["filler"] is not None and next(state["filler"], "end") == "end":
                state["filler"] = None

    def finish_filler():
        while state["filler"] is not None:
            fill()

    def split(src, hi, lo, *after, low_on=PO):
        th = on(SC, *after)(nc.scalar.activation, hi, src, ACT.Copy)
        e = prog.engines[low_on]
        tl = on(low_on, th, *after)(e.tensor_tensor, lo, src, hi.bitcast(F32), ALU.subtract)
        return th, tl

    def inverse_rms(dst, sums, dim, factor, *after):
        parts = sums.shape[0]
        bias = C("eps" if factor == 1 else f"eps{factor}", slice(0, parts))
        t = on(SC, *after)(nc.scalar.activation, dst, sums, ACT.Ln, bias=bias, scale=factor / dim)
        return on(SC, t)(nc.scalar.activation, dst, dst, ACT.Exp, scale=-0.5)

    norm = {}

    def restart_norms():
        norm.update(made=[None, None], summed=None, rs=None, read=None, readers=None, pending=None)

    def prepare(k, nt, gain, parts, done, his, lows, *h_free, at_start=False):
        xk, s, cols = x[:, k, TOK2 - nt:], k % 2, slice(TOK2 - nt, TOK2)
        if k == 0:
            norm["readers"] = prog.now(VE)
        before = norm["made"][s] if k else norm["read"]
        dst = sq[:, s, :nt] if k else sums[:, cols]
        if at_start:
            t = on(VE, before)(nc.vector.tensor_tensor, dst, xk, xk, ALU.mult)
        else:
            t = on(SC, done, before)(nc.scalar.activation, dst, xk, ACT.Square)
        if k:
            t = norm["made"][s] = on(PO, t, norm["summed"])(
                nc.gpsimd.tensor_tensor, sums[:, cols], sums[:, cols], sq[:, s, :nt], ALU.add)
        norm["summed"] = t
        hi, lo, g = parts[0][:, k, cols], parts[1][:, k, cols], gain[:, k:k + 1]
        th = on(SC, done, *h_free)(nc.scalar.activation, hi, xk, ACT.Copy, scale=g)
        his.append(th)
        lows.append(None)
        at = len(lows) - 1

        def lower():
            lows[at] = on(VE, th, *h_free)(nc.vector.scalar_tensor_tensor, lo, xk, g, hi.bitcast(F32),
                                           ALU.mult, ALU.subtract)
        later.append(lower)

    def finish_norm(nt, tiles=()):
        cols = slice(TOK2 - nt, TOK2)
        prog.wait(PE, free[TB_], norm["summed"])
        m = nc.tensor.matmul(ps[:, TB_, :nt], C("ones"), sums[:, cols], start=True, stop=True)
        for n, (a, _) in enumerate(tiles):
            m = nc.tensor.matmul(ps[:, TB_, nt + n:nt + n + 1], sums[:, a:a + 128], C("ones")[:, 0:1],
                                 start=True, stop=True)
        m = norm["read"] = prog.mark(PE, m)
        width = nt + len(tiles)
        out_ = rs[:, TOK2 - nt:TOK2 - nt + width]
        norm["rs"] = free[TB_] = inverse_rms(out_, ps[:, TB_, :width], D, 1, m, norm["readers"])

    def rs_of(nt):
        return rs[:, TOK2 - nt:TOK2]

    def project(u, kcs, act, nt, evacuate, his=(), lows=(), k0=0, width=128, last=False):
        if his:
            flush()
        w_hi, w_lo = stream.view(u, kcs)
        cut = slice(act[0].shape[2] - nt, act[0].shape[2])
        count = w_hi.shape[2] // width
        for c in range(count):
            b = next_bank()
            prog.wait(PE, free[b])
            cols = slice(c * width, (c + 1) * width)
            t = stream.product(u, ps[:, b, :nt],
                               [((w_hi[:, k, cols], w_lo[:, k, cols]),
                                 (act[0][:, k0 + k, cut], act[1][:, k0 + k, cut]), True) for k in range(kcs)],
                               his=his, lows=lows, tail=2 if his and c == 0 and kcs == KC else 0)
            if norm["pending"]:
                finish_norm(*norm["pending"])
                norm["pending"] = None
            leave(evacuate, c, b, t, ({0: (0, 1)} if last else {0: (0,), count // 2: (1,)}).get(c, ()))
            if kcs == KC or c % 2:
                fill()

    def project_tokens(u, kcs, act, tiles, cols, evacuate):
        w_hi, w_lo = stream.view(u, kcs)
        for n, (a, m) in enumerate(tiles):
            b = next_bank()
            prog.wait(PE, free[b])
            t = stream.product(u, ps[:, b, :cols],
                               [((act[0][:, k, a:a + 128], act[1][:, k, a:a + 128]),
                                 (w_hi[:, k, :cols], w_lo[:, k, :cols]), False) for k in range(kcs)])
            leave(evacuate, n, b, t, (n,) if n < 2 else ())
            fill()

    def track(evacuate, into):
        def wrapped(c, b, t):
            tok = evacuate(c, b, t)
            into.append(tok)
            return tok
        return wrapped

    def copy_to(dst, engine=SC, *more):
        def evacuate(c, b, t):
            d = dst(c)
            src = ps[:d.shape[0], b, :d.free_size()]
            if engine == SC:
                return on(SC, t, *more)(nc.scalar.activation, d, src, ACT.Copy)
            return on(VE, t, *more)(nc.vector.tensor_copy, d, src)
        return evacuate

    def normed_to(dst, nt, factor=1.0):
        def evacuate(c, b, t):
            d = dst(c)
            return on(VE, t, norm["rs"])(nc.vector.scalar_tensor_tensor, d, ps[:d.shape[0], b, :nt], factor,
                                         rs_of(nt)[:d.shape[0], :], ALU.mult, ALU.mult)
        return evacuate

    def normed_tokens_to(dst, tiles):
        def evacuate(c, b, t):
            d = dst(c)
            m = tiles[c][1]
            return on(SC, t, norm["rs"])(nc.scalar.activation, d, ps[:m, b, :d.free_size()], ACT.Copy,
                                         scale=rs[:m, TOK2 + c:TOK2 + c + 1])
        return evacuate

    def add_to_residual(nt, first, done, *then):
        def evacuate(c, b, t):
            k = first + c
            tok = on(VE, t)(nc.vector.tensor_tensor, x[:, k, TOK2 - nt:], x[:, k, TOK2 - nt:], ps[:, b, :nt], ALU.add)
            done.append(tok)
            prepare(k, nt, then[0], then[1], tok, *then[2:])
            return tok
        return evacuate

    def mlp(u, nt, his, lows, name, *then):
        with ExitStack() as own:
            f_hi, f_lo = (sbuf(f"{name}_ff_{n}", 128, FF // 128, nt, dt=F32R, into=own.enter_context)
                          for n in ("hi", "lo"))
            gone = prog.now(PE, SC, VE, PO)
            read, f_his, f_lows = [None, None], [], []

            def relu_squared(k, b, t):
                s = k % 2
                r = tmp[:, s, :nt]
                t1 = on(VE, t, norm["rs"], read[s])(nc.vector.scalar_tensor_tensor, r, ps[:, b, :nt], 0.0,
                                                    rs_of(nt), ALU.max, ALU.mult)
                if k == 0:
                    for e in (SC, VE, PO):
                        prog.wait(e, gone)
                th = on(SC, t1)(nc.scalar.activation, f_hi[:, k, :], r, ACT.Square)
                t2 = on(PO, th)(nc.gpsimd.tensor_tensor, r, r, r, ALU.mult)
                f_his.append(th)

                def end():
                    read[s] = on(VE, t2)(nc.vector.tensor_tensor, f_lo[:, k, :], r, f_hi[:, k, :].bitcast(F32), ALU.subtract)
                    f_lows.append(read[s])
                later.append(end)
                return t1
            for n in range(16):
                project(u + n, KC, (h_hi, h_lo), nt, lambda c, b, t, n=n: relu_squared(2 * n + c, b, t), his, lows)
            u += 16
            flush()
            done, h_read = [], prog.now(PE)
            for pair in range(4):
                banks = [next_bank(), next_bank()]
                for kb in range(4):
                    w = stream.view(u, KC)
                    for c, b in enumerate(banks):
                        if kb == 0:
                            prog.wait(PE, free[b])
                        cols = slice(c * 128, (c + 1) * 128)
                        ks = range(kb * KC, (kb + 1) * KC)
                        t = stream.product(u, ps[:, b, :nt],
                                           [((w[0][:, k - kb * KC, cols], w[1][:, k - kb * KC, cols]),
                                             (f_hi[:, k, :], f_lo[:, k, :]), True) for k in ks],
                                           start=kb == 0, stop=kb == 3, his=[f_his[k] for k in ks],
                                           lows=[f_lows[k] for k in ks])
                        if kb == 3:
                            halves = (c,) if pair < 3 else (0, 1) if c == 0 else ()
                            leave(add_to_residual(nt, 2 * pair, done, *then, *h_read), c, b, t, halves)
                        else:
                            flush()
                            later.append(stream.split_next(c))
                    u += 1
        return u

    def pipeline(items, scores, turn, apply):
        for k in range(len(items) + 2):
            if k >= 2:
                apply(items[k - 2])
            if k < len(items):
                scores(items[k])
            if 1 <= k <= len(items):
                turn(items[k - 1])
            yield

    COLS1 = [2048] * UNITS
    COLS1[10] = KC * 24

    def nsa_attention(B, t_in, t_gate, hid_rows, t_hid, ready):
        zq, zk, vtok, gate, hid = B["zq"], B["zk"], B["vtok"], B["gate"], B["hid"]
        t_norm, before = {}, []
        for name, view, gain, factor, src in (("q01", zq[:, 0:2, :], "g_q", 64, t_in["q"]),
                                              ("q23", zq[:, 2:4, :], "g_q", 64, t_in["q"]),
                                              ("k", zk[:, :, :], "g_k", 1, t_in["k"])):
            flat = view.rearrange("p a t -> p (a t)")
            s = on(SC, *src, *before)(nc.scalar.activation, sq[:, 0, :], flat, ACT.Square)
            yield
            m = on(PE, s, free[TB_])(nc.tensor.matmul, ps[:, TB_, :], C("blk64"), sq[:, 0, :], start=True, stop=True)
            r = inverse_rms(B["rn"][:, :], ps[:, TB_, :], 64, factor, m)
            free[TB_] = r
            t_norm[name] = on(VE, r)(nc.vector.scalar_tensor_tensor, flat, flat, P1(gain), B["rn"][:, :],
                                     ALU.mult, ALU.mult)
            before = [m, t_norm[name]]
            yield
        kc_ps, vc_ps = ps[:, TB_, 0:16], ps[0:16, TB_ + 1, 0:128]
        hid_done = []
        for kv in range(2):
            prog.wait(PE, free[TB_ + kv], t_hid[kv])
            for hc in range(2):
                m = nc.tensor.transpose(ps[:, TB_ + kv, 32 * hc:32 * hc + 32], hid_rows[:32, kv, 128 * hc:128 * hc + 128],
                                        C("ident")[:32, :32])
            m = prog.mark(PE, m)
            hid_done.append(on(SC, m)(nc.scalar.activation, hid[:, kv, :, :],
                                      ps[:, TB_ + kv, :64].rearrange("p (a b) -> p a b", a=2), ACT.Copy))
            free[TB_ + kv] = hid_done[-1]
        yield
        prog.wait(PE, *hid_done)
        for g in range(2):
            rows = slice(64 * g, 64 * g + 64)
            for hc in range(2):
                m = nc.tensor.matmul(kc_ps[rows, :], P1("w2_k")[:, hc * 64:hc * 64 + 64],
                                     hid[:, 0, hc, 16 * g:16 * g + 16], start=hc == 0, stop=hc == 1)
        t_k = prog.mark(PE, m)
        for g in range(2):
            for hc in range(2):
                m = nc.tensor.matmul(vc_ps[:, 64 * g:64 * g + 64], hid[:, 1, hc, 16 * g:16 * g + 16],
                                     P1("w2_v")[:, hc * 64:hc * 64 + 64], start=hc == 0, stop=hc == 1)
        t_v = prog.mark(PE, m)
        kcmp, vcmp = B["kcmp"], B["vcmp"]
        t1 = on(SC, t_k)(nc.scalar.activation, sq[:, 0, :16], kc_ps, ACT.Square)
        t2 = on(SC, t_k)(nc.scalar.activation, kcmp[:, :], kc_ps, ACT.Copy)
        t_vc = on(SC, t_v)(nc.scalar.activation, vcmp[:, :], vc_ps, ACT.Copy)
        free[TB_], free[TB_ + 1] = t2, t_vc
        yield
        m = on(PE, t1, t2)(nc.tensor.matmul, ps[:, TB_, :16], C("blk64"), sq[:, 0, :16], start=True, stop=True)
        r = inverse_rms(B["rn"][:, :16], ps[:, TB_, :16], 64, 1, m, *t_norm.values())
        free[TB_] = r
        t_kc = on(VE, r)(nc.vector.scalar_tensor_tensor, kcmp[:, :], kcmp[:, :], P1("g_k"), B["rn"][:, :16],
                         ALU.mult, ALU.mult)
        yield

        small = B["small"]
        turned = {"pt": None, "e": [None, None]}
        items = []
        for t in range(2):
            items.append({"t": t, "kind": "cmp"})
            items += [{"t": t, "kind": "keys", "br": br, "g": g} for br in range(2) for g in range(2)]
        for n, it in enumerate(items):
            it["n"] = n
        y_started = {}

        def scores(it):
            t, n = it["t"], it["n"]
            e = B["e"][:, n % 2, :]
            nm, sm, f = (small[:, n % 2, a, :] for a in range(3))
            prog.wait(PE, free[SB_], *t_norm.values(), t_kc)
            if it["kind"] == "cmp":
                s = ps[:, SB_:SB_ + 2, 0:64].rearrange("p g (j n) -> p g j n", j=4)
                for g in range(2):
                    rows = slice(64 * g, 64 * g + 64)
                    for j in range(4):
                        m = nc.tensor.matmul(s[:, g, j, :], zq[rows, j, 128 * t:128 * t + 128], kcmp[rows, :],
                                             start=True, stop=True)
                m = prog.mark(PE, m)
                ev = e[:, :128].rearrange("p (h n) -> p h n", h=8)
                neg = C("cmp_neg")[:, 16 * t:16 * t + 16].unsqueeze(1).unsqueeze(1).to_broadcast([128, 2, 4, 16])
                ok = C("cmp_01")[:, 16 * t:16 * t + 16].unsqueeze(1).to_broadcast([128, 8, 16])
                a = on(VE, m, turned["e"][n % 2])(nc.vector.tensor_tensor, e[:, :128].rearrange(
                    "p (g j n) -> p g j n", g=2, j=4), s, neg, ALU.add)
                free[SB_] = a
                a = on(VE, a)(nc.vector.reduce_max, nm, ev, AX, negate=True)
                a = on(VE, a)(nc.vector.tensor_tensor, ev, ev, nm.unsqueeze(2).to_broadcast([128, 8, 16]), ALU.add)
                a = on(SC, a)(nc.scalar.activation, e[:, :128], e[:, :128], ACT.Exp)
                a = on(VE, a)(nc.vector.tensor_tensor, ev, ev, ok, ALU.mult)
                a = on(VE, a)(nc.vector.reduce_sum, sm, ev, AX)
                a = on(VE, a)(nc.vector.tensor_scalar, sm, sm, 1e-30, None, ALU.max)
                a = on(VE, a)(nc.vector.reciprocal, f, sm)
                a = on(VE, a, t_gate)(nc.vector.tensor_tensor, f, f, gate[:, t, 0:8], ALU.mult)
                it["p"] = on(VE, a)(nc.vector.tensor_tensor, ev, ev, f.unsqueeze(2).to_broadcast([128, 8, 16]), ALU.mult)
                return
            L, br, g = 128 * (t + 1), it["br"], it["g"]
            rows = slice(64 * g, 64 * g + 64)
            s = ps[:, SB_:SB_ + 2, :].rearrange("p b c -> p (b c)")[:, :4 * L].rearrange("p (j l) -> p j l", j=4)
            for j in range(4):
                nc.tensor.matmul(s[:, j, :], zq[rows, j, 128 * t:128 * t + 128], zk[rows, br, :L], start=True, stop=False)
                m = nc.tensor.matmul(s[:, j, L - 128:], ident_b[:, :], causal_b[:, :], start=False, stop=True)
            m = prog.mark(PE, m)
            a = on(VE, m)(nc.vector.reduce_max, nm[:, :4], s, AX, negate=True)
            ev = e[:, :4 * L].rearrange("p (j l) -> p j l", j=4)
            prog.wait(SC, a, turned["e"][n % 2])
            for j in range(4):
                b = on(SC)(nc.scalar.activation, ev[:, j, :], s[:, j, :], ACT.Exp, bias=nm[:, j:j + 1],
                           accum_out=sm[:, j:j + 1])
            free[SB_] = [a, b]
            a = on(VE, b)(nc.vector.reciprocal, f[:, :4], sm[:, :4])
            c0 = (1 + br) * 8 + 4 * g
            a = on(VE, a, t_gate)(nc.vector.tensor_tensor, f[:, :4], f[:, :4], gate[:, t, c0:c0 + 4], ALU.mult)
            wide = f[:, :4].unsqueeze(2).to_broadcast([128, 4, L])
            it["p"] = [on(e_, a)(prog.engines[e_].tensor_tensor, ev[:, js, :], ev[:, js, :], wide[:, js, :], ALU.mult)
                       for e_, js in ((PO, slice(3, 4)), (VE, slice(0, 3)))]

        def turn(it):
            n, t = it["n"], it["t"]
            e, pt = B["e"][:, n % 2, :], B["pt"]
            prog.wait(PE, it["p"], free[TB_], free[TB_ + 1])
            if it["kind"] == "cmp":
                for h in range(8):
                    m = nc.tensor.transpose(ps[:16, TB_ + h // 4, h % 4 * 128:h % 4 * 128 + 128],
                                            e[:, 16 * h:16 * h + 16], C("ident"))
                m = prog.mark(PE, m)
                it["pt"] = on(VE, m, turned["pt"])(nc.vector.tensor_copy, pt[:16, :, :], ps[:16, TB_:TB_ + 2, :])
                free[TB_] = free[TB_ + 1] = it["pt"]
            else:
                L = 128 * (t + 1)
                ev = e[:, :4 * L].rearrange("p (j l) -> p j l", j=4)
                done = []
                for kc in range(t + 1):
                    for j in range(4):
                        m = nc.tensor.transpose(ps[:, TB_ + kc, 128 * j:128 * j + 128],
                                                ev[:, j, 128 * kc:128 * kc + 128], C("ident"))
                    m = prog.mark(PE, m)
                    if kc == 0:
                        c = on(VE, m, turned["pt"])(nc.vector.tensor_copy, pt[:, kc, :], ps[:, TB_ + kc, :])
                    else:
                        c = on(SC, m, turned["pt"])(nc.scalar.activation, pt[:, kc, :], ps[:, TB_ + kc, :], ACT.Copy)
                    free[TB_ + kc] = c
                    done.append(c)
                it["pt"] = done
            turned["e"][n % 2] = m

        def apply(it):
            t, pt = it["t"], B["pt"]
            prog.wait(PE, it["pt"], t_vc, t_in["v"])
            if it["kind"] == "cmp":
                prog.wait(PE, free[YB_])
                for g in range(2):
                    m = nc.tensor.matmul(ps[64 * g:64 * g + 64, YB_, :], vcmp[:, 64 * g:64 * g + 64], pt[:16, g, :],
                                         start=True, stop=True, skip_group_check=True)
            else:
                br, g = it["br"], it["g"]
                for kc in range(t + 1):
                    v = vtok[:, kc, 128 * br + 64 * g:128 * br + 64 * g + 64]
                    m = nc.tensor.matmul(ps[64 * g:64 * g + 64, YB_, :], v, pt[:, kc, :], start=False,
                                         stop=True, skip_group_check=True)
            m = turned["pt"] = prog.mark(PE, m)
            if it["kind"] == "keys" and it["br"] == 1 and it["g"] == 1:
                y = B["yn"][:, :, 128 * t:128 * t + 128]
                c = on(SC, m)(nc.scalar.activation, y, ps[:, YB_, :].rearrange("p (j q) -> p j q", j=4), ACT.Copy)
                free[YB_] = c
                th, tl = split(y, B["yn_hi"][:, :, 128 * t:128 * t + 128], B["yn_lo"][:, :, 128 * t:128 * t + 128], c)
                B["yn_hi_done"].append(th)
                B["yn_lo_done"].append(tl)

        yield from pipeline(items, scores, turn, apply)
        while not ready["ret"]:
            yield
        yield from retention(B)

    def retention(B):
        rq, rk, rv, yr, rot = B["rq"], B["rk"], B["rv"], B["yr"], B["rot"]
        t_rope = []
        for r in (rq, rk):
            for pair in range(2):
                v = r[:, 2 * pair:2 * pair + 2, :]
                cos, sin = (C(c).unsqueeze(1).to_broadcast([128, 2, SEQ]) for c in ("cos_ret", "sin_ret"))
                m = on(PE, free[TB_], B["t_r"])(nc.tensor.matmul, ps[:, TB_, :], C("rot_ret"),
                                               v.rearrange("p a t -> p (a t)"), start=True, stop=True)
                a = on(VE, m, *t_rope[-1:])(nc.vector.tensor_tensor, rot[:, :, :],
                                            ps[:, TB_, :].rearrange("p (a t) -> p a t", a=2), sin, ALU.mult)
                free[TB_] = a
                b = on(VE, m)(nc.vector.tensor_tensor, v, v, cos, ALU.mult)
                t_rope.append(on(VE, a, b)(nc.vector.tensor_tensor, v, v, rot[:, :, :], ALU.add))
                yield
        read = [None, None]

        def scores(h):
            prog.wait(PE, free[SB_], *t_rope)
            nc.tensor.matmul(ps[:, SB_, 0:256], rk[:, h, 0:128], rq[:, h, :], start=True, stop=True)
            m = on(PE)(nc.tensor.matmul, ps[:, SB_, 256:384], rk[:, h, 128:256], rq[:, h, 128:256], start=True, stop=True)
            B[f"a{h}"] = on(VE, m, read[h % 2])(nc.vector.tensor_tensor, B["e"][:, h % 2, :384], ps[:, SB_, :384],
                                               C("decay")[:, 384 * h:384 * h + 384], ALU.mult)
            free[SB_] = B[f"a{h}"]

        def turn(h):
            a, e = slice(128 * h, 128 * h + 128), B["e"][:, h % 2, :]
            prog.wait(PE, free[YB_], B[f"a{h}"], *B["t_rv"])
            nc.tensor.matmul(ps[:, YB_, :256], rv[:, 0, a], e[:, 0:256], start=True, stop=True, skip_group_check=True)
            m = on(PE)(nc.tensor.matmul, ps[:, YB_, 128:256], rv[:, 1, a], e[:, 256:384], start=False, stop=True,
                       skip_group_check=True)
            read[h % 2] = m
            c = on(SC, m)(nc.scalar.activation, yr[:, h, :], ps[:, YB_, :256], ACT.Copy)
            free[YB_] = B[f"y{h}"] = on(SC, c, B.get(f"m{h - 2}"))(nc.scalar.activation, sq[:, h % 2, :256], ps[:, YB_, :256], ACT.Square)

        def apply(h):
            m = B[f"m{h}"] = on(PE, free[TB_], B[f"y{h}"])(nc.tensor.matmul, ps[:, TB_, :256], C("ones"), sq[:, h % 2, :256],
                                                          start=True, stop=True)
            r = inverse_rms(B["rn"][:, :256], ps[:, TB_, :256], 128, 1, m, *B["yr_done"][-1:])
            free[TB_] = r
            B["yr_done"].append(on(VE, r)(nc.vector.tensor_tensor, yr[:, h, :], yr[:, h, :], B["rn"][:, :256], ALU.mult))

        yield from pipeline(list(range(4)), scores, turn, apply)

    def first_layer(i):
        nt, act = SEQ, (h_hi, h_lo)
        tiles = [(META, 128), (META + 128, 128)]
        stream.start_layer(i, COLS1)
        nc.scalar.dma_start(params[:, :n_par1], ins["params1"][bass.ds(i, 1)].rearrange("a p n -> (a p) n"))\
            .then_inc(loaded, 16)
        norm["pending"] = (nt, tiles)
        with ExitStack() as own:
            keep = own.enter_context

            def buf(name, *shape, dt=F32, into=keep):
                return sbuf("b1_" + name, 128, *shape, dt=dt, into=into)

            merge = buf("merge", 16, nt)
            at_end = {n: buf(n, 4, nt) for n in ("rg", "yr")}
            at_end.update({n: buf(n, 4, nt, dt=F32R) for n in ("yn_hi", "yn_lo")})
            at_end["e"] = buf("e", 2, 1024)
            inner = ExitStack()

            def tmp_buf(name, *shape):
                return buf(name, *shape, into=inner.enter_context)

            B = {"zq": tmp_buf("zq", 4, nt), "zk": tmp_buf("zk", 2, nt), "vtok": tmp_buf("vtok", 2, 256),
                 "gate": tmp_buf("gate", 2, 24), "pt": tmp_buf("pt", 2, 512),
                 "small": tmp_buf("small", 2, 3, 8), "rn": tmp_buf("rn", 512), "rot": tmp_buf("rot", 2, nt),
                 "hid": tmp_buf("hid", 2, 2, 32), "kcmp": tmp_buf("kcmp", 16),
                 "vcmp": sbuf("b1_vcmp", 16, 128, into=inner.enter_context), "yn": tmp_buf("yn", 4, nt),
                 "rq": tmp_buf("rq", 4, nt), "rk": tmp_buf("rk", 4, nt), "rv": tmp_buf("rv", 2, 512),
                 "yn_hi_done": [], "yn_lo_done": [], "yr_done": [], "t_rv": [], **at_end}
            place = merge[:, :, :].rearrange("p c t -> p (c t)")
            n_s = 4 * (nt + 16)
            shifted = place[:, :n_s].rearrange("p (a t) -> p a t", a=4)
            z32 = place[:, n_s:n_s + 1024].rearrange("p (a n) -> p a n", a=2)
            scratch = place[:, n_s + 1024:n_s + 1792].rearrange("p (a n) -> p a n", a=3)
            hid_rows = place[:, n_s + 1792:n_s + 2304].rearrange("p (a n) -> p a n", a=2)
            z_hi, z_lo = (B[f"yn_{n}"][:, :, :].rearrange("p (a b) t -> p a (b t)", a=2) for n in ("hi", "lo"))
            z_done, t_hid, t_in = [], [], {"q": [], "k": [], "v": []}
            for kv in range(2):
                built = []

                def evacuate(g, b, t, kv=kv, built=built):
                    s, r = shifted[:, 2 * kv + g, :], rs_of(nt)
                    u = on(VE, t, norm["rs"])(nc.vector.tensor_tensor, s[0:64, 0:nt], ps[0:64, b, 0:nt], r[0:64, :], ALU.mult)
                    v = on(VE)(nc.vector.tensor_tensor, s[64:128, 0:nt - 1], ps[64:128, b, 1:nt], r[64:128, 1:nt], ALU.mult)
                    w = on(SC, v, norm["rs"])(nc.scalar.activation, s[64:128, nt - 1:nt + 16], ps[64:128, b, nt - 1:nt]
                                  .to_broadcast([64, 17]), ACT.Copy, scale=r[64:128, nt - 1:nt])
                    c = on(SC, u)(nc.scalar.activation, s[0:64, nt:nt + 16], s[0:64, nt - 1:nt].to_broadcast([64, 16]), ACT.Copy)
                    out_ = z32[:, kv, :].rearrange("p (c g n) -> p c g n", c=16, g=2)
                    for half, e in ((0, VE), (1, PO)):
                        src = s[:, 16 * half:16 * half + nt].rearrange("p (n c two) -> p c n two", c=8, two=2)[:, :, :, 0]
                        pos = P1("pos_k" if kv == 0 else "pos_v")[:, 8 * half:8 * half + 8]
                        if not built[1:]:
                            prog.engines[e].wait_ge(loaded, 16)
                        built.append(on(e, c, v)(prog.engines[e].tensor_tensor, out_[:, 8 * half:8 * half + 8, g, :], src,
                                                 pos.unsqueeze(2).to_broadcast([128, 8, 16]), ALU.add))
                    return [v, w]

                project(kv, KC, act, nt, evacuate)
                z_done.append(split(z32[:, kv, :], z_hi[:, kv, :], z_lo[:, kv, :], *built))
            t_neg = on(VE, norm["rs"])(nc.vector.tensor_scalar, neg_rs[:, :], rs[:, TOK2:TOK2 + 2], -1.0, None, ALU.mult)
            for e in (SC, PE):
                prog.engines[e].wait_ge(loaded, 16)

            def compress(u, kv, half):
                w_hi, w_lo = stream.view(u, KC)
                b, zs = SB_ + kv, [slice(32 * c, 32 * c + 32) for c in range(8 * half, 8 * half + 8)]
                prog.wait(PE, free[b])
                t = stream.product(u, ps[:32, b, :256],
                                   [((z_hi[:, kv, zs[c]], z_lo[:, kv, zs[c]]), (w_hi[:, c, :], w_lo[:, c, :]), False)
                                    for c in range(KC)], start=half == 0, stop=half == 1,
                                   his=[z_done[kv][0]] * KC, lows=[z_done[kv][1]] * KC)
                flush()
                for h in range(2):
                    later.append(stream.split_next(h))
                if half == 0:
                    return
                zc, z2, ez = (scratch[:32, a, :] for a in range(3))
                a = on(SC, t, *t_hid)(nc.scalar.activation, zc, ps[:32, b, :256], ACT.Copy)
                c = on(SC, t, *t_hid)(nc.scalar.activation, z2, ps[:32, b, :256], ACT.Square)
                free[b] = c
                d = on(PO, c)(nc.gpsimd.tensor_scalar, z2, z2, 0.044715, 1.0, ALU.mult, ALU.add)
                d = on(PO, a, d)(nc.gpsimd.tensor_tensor, z2, z2, zc, ALU.mult)
                d = on(SC, d)(nc.scalar.activation, ez, z2, ACT.Exp, scale=-2.0 * float(np.sqrt(2.0 / np.pi)))
                d = on(VE, d)(nc.vector.tensor_scalar, ez, ez, 1.0, None, ALU.add)
                d = on(VE, d)(nc.vector.reciprocal, ez, ez)
                t_hid.append(on(PO, d)(nc.gpsimd.tensor_tensor, hid_rows[:32, kv, :], zc, ez, ALU.mult))

            project(2, KC, act, nt, track(normed_to(lambda c: B["zq"][:, c, :], nt), t_in["q"]))
            compress(3, 0, 0)
            project(4, KC, act, nt, track(normed_to(lambda c: B["zq"][:, 2 + c, :], nt), t_in["q"]))
            compress(5, 0, 1)
            project(6, KC, act, nt, track(normed_to(lambda c: B["zk"][:, c, :], nt), t_in["k"]))
            compress(7, 1, 0)
            project_tokens(8, KC, act, tiles, 256, track(normed_tokens_to(lambda c: B["vtok"][:, c, :], tiles), t_in["v"]))
            compress(9, 1, 1)
            gates = []

            def gate_out(c, b, t):
                g = B["gate"][:, c, :]
                e = on(SC, t, t_neg)(nc.scalar.activation, g, ps[:, b, 0:24], ACT.Exp, scale=neg_rs[:, c:c + 1])
                a = on(VE, e)(nc.vector.tensor_scalar, g, g, 1.0, None, ALU.add)
                gates.append(on(VE, a)(nc.vector.reciprocal, g, g))
                return e
            project_tokens(10, KC, act, tiles, 24, gate_out)
            ready = {"ret": False}
            for e in (SC, VE, PE):
                prog.engines[e].wait_ge(consts_in, 16)
            state["filler"] = nsa_attention(B, t_in, gates[-1], hid_rows, t_hid, ready)
            t_r = []
            for n in range(2):
                project(11 + n, KC, act, nt, track(normed_to(lambda c, n=n: B["rq"][:, 2 * n + c, :], nt), t_r))
            for n in range(2):
                project(13 + n, KC, act, nt, track(normed_to(lambda c, n=n: B["rk"][:, 2 * n + c, :], nt), t_r))
            for n in range(2):
                cols = slice(256 * n, 256 * n + 256)
                project_tokens(15 + n, KC, act, tiles, 256,
                               track(normed_tokens_to(lambda c, cols=cols: B["rv"][:, c, cols], tiles), B["t_rv"]))
            t_g = []
            for n in range(2):
                project(17 + n, KC, act, nt, track(normed_to(lambda c, n=n: B["rg"][:, 2 * n + c, :], nt), t_g))
            B["t_r"] = t_r
            ready["ret"] = True
            t_m = []
            for n in range(8):
                project(19 + n, KC, act, nt, track(normed_to(lambda c, n=n: merge[:, 2 * n + c, :], nt), t_m))
            finish_filler()
            sig = B["e"][:, 0, :].rearrange("p (h t) -> p h t", h=4)
            t_s, t_rg = {}, []
            h_read = prog.now(PE)

            def sigmoid(k):
                if k == "rg":
                    t_rg.append(on(SC, *t_g, h_read)(nc.scalar.activation, sig, B["rg"][:, :, :], ACT.Sigmoid))
                else:
                    t_s[k] = on(SC, t_m[k])(nc.scalar.activation, merge[:, k, :], merge[:, k, :], ACT.Sigmoid)

            for k in range(4):
                sigmoid(k)
            to_come = [[4, 5], [6, 7], ["rg"], [8, 9], [10, 11], [12, 13], [14, 15]]

            def merge_nsa(n):
                def evacuate(c, b, t):
                    m = merge[:, 4 * n + c, :]
                    for k in to_come.pop(0) if to_come else ():
                        sigmoid(k)
                    return on(VE, t, t_s[4 * n + c])(nc.vector.tensor_tensor, m, m, ps[:, b, :nt], ALU.mult)
                return evacuate

            mixed = []

            def merge_ret(n):
                def evacuate(c, b, t):
                    m, r = merge[:, 4 * n + c, :], merge[:, 8 + 4 * n + c, :]
                    a = on(VE, t, t_s[8 + 4 * n + c])(nc.vector.tensor_tensor, r, r, ps[:, b, :nt], ALU.mult)
                    mixed.append(on(PO, a)(nc.gpsimd.tensor_tensor, m, m, r, ALU.add))
                    return a
                return evacuate

            for n in range(2):
                project(27 + n, 4, (B["yn_hi"], B["yn_lo"]), nt, merge_nsa(n), [B["yn_hi_done"]] * 4, [B["yn_lo_done"]] * 4)
                if n == 0:
                    a = on(PO, *t_rg)(nc.gpsimd.tensor_tensor, sig, sig, B["rg"][:, :, :], ALU.mult)
                    a = on(VE, a, *B["yr_done"])(nc.vector.tensor_tensor, B["yr"][:, :, :], B["yr"][:, :, :], sig, ALU.mult)
                    r_his, r_lows = split(B["yr"][:, :, :], h_hi[:, 4:8, META:], h_lo[:, 4:8, META:], a, *h_read)
            nc.scalar.preload_act_table_set("natural_log_exp_and_others")
            for n in range(2):
                project(29 + n, 4, act, nt, merge_ret(n), [r_his] * 4, [r_lows] * 4, k0=4)
            flush()
            inner.close()
            mix = [buf(f"mix_{n}", KC, nt, dt=F32R) for n in ("hi", "lo")]
            h_read = prog.now(PE)
            for e in (SC, VE, PO):
                prog.wait(e, prog.now(PE, VE))
            his, lows = [], []
            for k in range(KC):
                th, tl = split(merge[:, k, :], mix[0][:, k, :], mix[1][:, k, :], mixed[k], low_on=VE if k % 2 else PO)
                his.append(th)
                lows.append(tl)
            x_done, next_his, next_lows = [], [], []
            for n in range(4):
                project(31 + n, KC, mix, nt, add_to_residual(nt, 2 * n, x_done, P1("g_mlp"), act, next_his, next_lows,
                                                             *h_read), his, lows)
        norm["pending"] = (nt,)
        with ExitStack() as own:
            h2 = [sbuf(f"b1_h2_{n}", 128, KC, TOK2, dt=F32R, into=own.enter_context) for n in ("hi", "lo")]
            p_hi, p_lo = (sbuf(f"b1_p_{n}", 128, 2, nt, dt=F32R, into=own.enter_context) for n in ("hi", "lo"))
            p = P1("p").rearrange("q (k t) -> q k t", k=2)
            t_split = split(p, p_hi[:, :, :], p_lo[:, :, :], prog.now(PE, SC, VE, PO))
            his, lows = [], []
            u = mlp(35, nt, next_his, next_lows, "b1", P1("g_ple"), h2, his, lows)
            ple = sbuf("b1_ple", 128, KC, nt, into=own.enter_context)
            prog.wait(VE, prog.now(PE))
            t_p = []
            project(u, 2, (p_hi, p_lo), nt, track(copy_to(lambda c: ple[:, c, :], VE), t_p), [t_split[0]] * 2, [t_split[1]] * 2)
            u += 1
            norm["pending"] = (nt,)
            used = [None, None]

            def gated(n):
                def evacuate(c, b, t):
                    k = 2 * n + c
                    g = tmp[:, k % 2, :nt]
                    a = on(VE, t, norm["rs"], used[k % 2])(nc.vector.tensor_tensor, g, ps[:, b, :nt], rs_of(nt), ALU.mult)
                    d = on(SC, a)(nc.scalar.activation, g, g, ACT.Sigmoid)

                    def end():
                        e = on(VE, d, *t_p)(nc.vector.tensor_tensor, g, g, ple[:, k, :], ALU.mult)
                        used[k % 2] = on(VE, e)(nc.vector.tensor_tensor, x[:, k, META:], x[:, k, META:], g, ALU.add)
                        prepare(k, nt, P1("g_next"), act, used[k % 2], [], [])
                    later.append(end)
                    return a
                return evacuate

            for n in range(4):
                project(u, KC, h2, nt, gated(n), his, lows, last=n == 3)
                u += 1
            flush()
            nc.scalar.preload_act_table_set("natural_log_exp_and_others")
            assert u == UNITS

    COLS2 = [2048] * UNITS
    COLS2[7] = 1024
    COLS2[8:10] = [16, 16]

    TILES = [(META, 128), (META + 128, 128), (0, META)]
    SEEN = [[2, 0], [2, 0, 1], [2]]

    def sums_of_squares(rows, ones, squares, *after):
        prog.wait(PE, free[SB_], *after)
        for s in range(2):
            m = nc.tensor.matmul(ps[rows, SB_ + s, :TOK2], C(ones, rows)[:, :rows.stop], squares[:, s, :],
                                 start=True, stop=True)
        return prog.mark(PE, m)

    def wide(z, rows):
        return z.unsqueeze(1).to_broadcast([rows.stop - rows.start, 2, TOK2])

    def rope_norms(todo, rows, ones, names, dim, factor_of, B):
        rn, rot, sq2 = B["rn"][rows, :, :], B["rot"][rows, :, :], sq[rows, :, :TOK2]
        _, cos, sin = (C(n, rows) for n in names)
        last, squared = {"sq": None, "rot": None, "rn": None}, None

        def square(n):
            return on(SC, *todo[n][3], last["sq"])(nc.scalar.activation, sq2, todo[n][0], ACT.Square)

        squared = square(0)
        yield
        for n, (v, gain, turned_gain, toks) in enumerate(todo):
            m0 = last["sq"] = sums_of_squares(rows, ones, sq2, squared)
            prog.wait(PE, free[TB_], free[TB_ + 1], *toks, *B["gains_done"])
            for s in range(2):
                m = nc.tensor.matmul(ps[rows, TB_ + s, :TOK2], turned_gain[rows, :rows.stop], v[:, s, :], start=True, stop=True)
            m1 = prog.mark(PE, m)
            r = free[SB_] = inverse_rms(rn, ps[rows, SB_:SB_ + 2, :TOK2], dim, factor_of(n), m0, last["rn"])
            a = on(VE, m1, last["rot"])(nc.vector.tensor_tensor, rot, ps[rows, TB_:TB_ + 2, :TOK2], wide(sin, rows), ALU.mult)
            free[TB_] = free[TB_ + 1] = a
            c = on(VE, m1, m0)(nc.vector.scalar_tensor_tensor, v, v, gain, wide(cos, rows), ALU.mult, ALU.mult)
            a = last["rot"] = on(PO, a, c)(nc.gpsimd.tensor_tensor, v, v, rot, ALU.add)
            last["rn"] = on(VE, a, r)(nc.vector.tensor_tensor, v, v, rn, ALU.mult)
            if n + 1 < len(todo):
                squared = square(n + 1)
            yield
        B["normed"] = [last["rn"]]

    def softmax_attention(B, query, key, value, width, combine, meta_done, finish, toks):
        e, pt, ptm, small = B["e"], B["pt"], B["ptm"], B["small"]
        items = [{"g": None, "t": 2}] + [{"g": g, "t": t} for g in range(4) for t in (1, 0)]
        for n, it in enumerate(items):
            it["n"] = n
        turned = {"e": [None, None], "pt": None}

        def meta_scores(it):
            prog.wait(PE, free[SB_], *toks)
            for s in range(2):
                for g in range(4):
                    nc.tensor.matmul(ps[:META, SB_ + s, 16 * g:16 * g + 16], query(g, s)[:, :META], key(g, s)[:, :META],
                                     start=True, stop=False, skip_group_check=True)
                    a = nc.tensor.matmul(ps[:META, SB_ + s, 16 * g:16 * g + 16], ident_b[:META, :META],
                                         causal_b[:META, :META], start=False, stop=True, skip_group_check=True)
            a = prog.mark(PE, a)
            S = ps[:META, SB_:SB_ + 2, :64].rearrange("p s (g k) -> p s g k", g=4)
            E = e[:META, it["n"] % 2, :, :64].rearrange("p s (g k) -> p s g k", g=4)
            nm, sm, f = (small[:META, it["n"] % 2, c, :].rearrange("p (s g) -> p s g", s=2) for c in range(3))
            over = lambda z: z.unsqueeze(3).to_broadcast([META, 2, 4, META])
            a = on(VE, a)(nc.vector.reduce_max, nm, S, AX, negate=True)
            a = free[SB_] = on(VE, a)(nc.vector.tensor_tensor, E, S, over(nm), ALU.add)
            a = on(SC, a)(nc.scalar.activation, E, E, ACT.Exp)
            a = on(VE, a)(nc.vector.reduce_sum, sm, E, AX)
            a = on(VE, a)(nc.vector.reciprocal, f, sm)
            if width == 1:
                a = on(VE, a)(nc.vector.tensor_scalar, f[:, 1, :], f[:, 1, :], B["neg_lam"][:META, :], None, ALU.mult)
            a = on(VE, a)(nc.vector.tensor_tensor, E, E, over(f), ALU.mult)
            if width == 1:
                a = on(VE, a)(nc.vector.tensor_tensor, E[:, 0], E[:, 0], E[:, 1], ALU.add)
            it["p"] = a

        def scores(it):
            g, t, n = it["g"], it["t"], it["n"]
            if t == 2:
                return meta_scores(it)
            q0, m = TILES[t]
            L = q0 + m
            prog.wait(PE, free[SB_], *toks)
            for s in range(2):
                q, k = query(g, s)[:, q0:q0 + m], key(g, s)
                bank = ps[:m, SB_ + s, :]
                nc.tensor.matmul(bank[:, :L], q, k[:, :L], start=True, stop=False)
                a = nc.tensor.matmul(bank[:, q0:L], ident_b[:m, :m], causal_b[:m, :m], start=False, stop=True)
            a = prog.mark(PE, a)
            S, E = ps[:m, SB_:SB_ + 2, :L], e[:m, n % 2, :, :L]
            nm, sm, f = (small[:m, n % 2, c, :2] for c in range(3))
            a = on(VE, a)(nc.vector.reduce_max, nm, S, AX, negate=True)
            prog.wait(SC, a, turned["e"][n % 2])
            for s in range(2):
                b = on(SC)(nc.scalar.activation, E[:, s, :], S[:, s, :], ACT.Exp, bias=nm[:, s:s + 1],
                           accum_out=sm[:, s:s + 1])
            free[SB_] = [a, b]
            a = on(VE, b)(nc.vector.reciprocal, f, sm)
            it["p"] = combine(E, f, a, m, L)

        def turn(it):
            t, n = it["t"], it["n"]
            m = TILES[t][1]
            prog.wait(PE, it["p"], free[TB_], free[TB_ + 1])
            if t == 2:
                for s in range(width):
                    for g in range(4):
                        a = nc.tensor.transpose(ps[:META, TB_ + 1, 64 * s + 16 * g:64 * s + 16 * g + 16],
                                                e[:META, n % 2, s, 16 * g:16 * g + 16], C("ident")[:META, :META])
                a = turned["e"][n % 2] = prog.mark(PE, a)
                it["pt"] = on(SC, a, turned["pt"])(nc.scalar.activation, ptm[:, :64 * width], ps[:META, TB_ + 1, :64 * width], ACT.Copy)
                free[TB_ + 1] = it["pt"]
                return
            for s in range(width):
                for kt in SEEN[t]:
                    c0, w = TILES[kt]
                    dst = (ps[:w, TB_ + 1, 128 * s:128 * s + m] if kt == 2
                           else ps[:, TB_, 256 * s + 128 * kt:256 * s + 128 * kt + m])
                    a = nc.tensor.transpose(dst, e[:m, n % 2, s, c0:c0 + w], C("ident")[:m, :m])
            a = turned["e"][n % 2] = prog.mark(PE, a)
            done = []
            view = [z.rearrange("p (s k c) -> p s k c", s=2, k=2)[:, :width, :t + 1, :] for z in (pt, ps[:, TB_, :])]
            done.append(on(VE, a, turned["pt"])(nc.vector.tensor_copy, view[0], view[1]))
            done.append(on(SC, a, turned["pt"])(nc.scalar.activation, ptm[:, :128 * width], ps[:META, TB_ + 1, :128 * width], ACT.Copy))
            free[TB_] = free[TB_ + 1] = it["pt"] = done

        def apply(it):
            g, t = it["g"], it["t"]
            q0, m = TILES[t]
            prog.wait(PE, it["pt"])
            if t != 0:
                prog.wait(PE, free[YB_])
            for s in range(width):
                rows = slice(64 * s, 64 * s + 64) if width == 2 else slice(0, 128)
                if t == 2:
                    for h in range(4):
                        a = nc.tensor.matmul(ps[rows, YB_, 16 * h:16 * h + 16], value(h, s, 2),
                                             ptm[:, 64 * s + 16 * h:64 * s + 16 * h + 16], start=True, stop=True,
                                             skip_group_check=True)
                    continue
                for c, kt in enumerate(SEEN[t]):
                    p = ptm[:, 128 * s:128 * s + m] if kt == 2 else pt[:, 256 * s + 128 * kt:256 * s + 128 * kt + m]
                    a = nc.tensor.matmul(ps[rows, YB_, q0:q0 + m], value(g, s, kt), p, start=c == 0, stop=True,
                                         skip_group_check=True)
            a = turned["pt"] = prog.mark(PE, a)
            if t == 2:
                free[YB_] = meta_done(ps[:, YB_, :64].rearrange("p (g t) -> p g t", g=4), a)
            elif t == 0:
                free[YB_] = finish(g, a)

        yield from pipeline(items, scores, turn, apply)

    def output(B, at, src, *after):
        assert not B["o_busy"], "products with the branch before are still to come"
        hi, lo = B["o_hi"][at], B["o_lo"][at]
        th = on(SC, *after, *B["o_read"])(nc.scalar.activation, hi, src, ACT.Copy)
        tl = on(VE, th, *after, *B["o_read"])(nc.vector.tensor_tensor, lo, src, hi.bitcast(F32), ALU.subtract)
        B["o_his"].append(th)
        B["o_lows"].append(tl)
        return tl

    ALL = slice(None)
    META_PART = (ALL, ALL, slice(0, META))

    def mla(B, heads, t_v, t_d):
        mq, mk, mv, kr = B["mq"], B["mk"], B["mv"], B["kr"]
        rows, up, low = slice(0, 96), slice(64, 96), slice(0, 64)
        names = ("rot_mla", "cos_mla", "sin_mla")
        ksq, rn = B["ksq"], B["rn_k"]
        q_steps = rope_norms([(mq[:96, 2 * h:2 * h + 2, :], P2("g_q", rows), B["rot_q"], heads["q"]) for h in range(4)],
                             rows, "ones", names, 96, lambda n: 96, B)
        a = on(SC, *heads["kr"])(nc.scalar.activation, ksq[up, 0, :], kr[up, :], ACT.Square)
        b = on(SC, a)(nc.scalar.activation, ksq[up, 1, :], kr[up, :], ACT.Square)
        g = on(VE, b)(nc.vector.tensor_scalar, kr[up, :], kr[up, :], P2("g_k", up), None, ALU.mult)
        next(q_steps)
        yield
        m = on(PE, g, free[YB_])(nc.tensor.matmul, ps[:96, YB_, :TOK2], C("rot_mla", up)[:, :96], kr[up, :],
                                 start=True, stop=True)
        a = on(VE, m)(nc.vector.tensor_tensor, B["rot_k"][up, :], ps[up, YB_, :TOK2], C("sin_mla", up), ALU.mult)
        free[YB_] = a
        c = on(VE, m)(nc.vector.tensor_tensor, kr[up, :], kr[up, :], C("cos_mla", up), ALU.mult)
        roped = on(VE, a, c)(nc.vector.tensor_tensor, kr[up, :], kr[up, :], B["rot_k"][up, :], ALU.add)
        last, m = [], None
        for n in range(4):
            next(q_steps, None)
            pair = slice(2 * n, 2 * n + 2)
            a = on(SC, m, *heads["k"])(nc.scalar.activation, ksq[low, :, :], mk[low, pair, :], ACT.Square)
            yield
            m = sums_of_squares(rows, "ones", ksq, a, b)
            r = free[SB_] = inverse_rms(rn, ps[:96, SB_:SB_ + 2, :TOK2], 96, 1, m, last)
            c = on(VE, r)(nc.vector.scalar_tensor_tensor, mk[low, pair, :], mk[low, pair, :], P2("g_k", low),
                          rn[low, :, :], ALU.mult, ALU.mult)
            d = on(VE, r, roped)(nc.vector.tensor_tensor, mk[up, pair, :], wide(kr[up, :], up), rn[up, :, :], ALU.mult)
            last = [c, d]
            yield
        next(q_steps, None)
        ready = B["normed"] + last + t_v

        def combine(E, f, a, m, L):
            return on(VE, a)(nc.vector.tensor_tensor, E, E, f.unsqueeze(2).to_broadcast([m, 2, L]), ALU.mult)

        yield from softmax_attention(
            B, lambda g, s: mq[:96, 2 * g + s, :], lambda g, s: mk[:96, 2 * g + s, :],
            lambda g, s, kt: mv[:TILES[kt][1], kt, 128 * g + 64 * s:128 * g + 64 * s + 64], 2, combine,
            lambda src, a: output(B, META_PART, src, a),
            lambda g, a: output(B, (ALL, g, slice(META, TOK2)), ps[:, YB_, META:TOK2], a), ready)
        names = ("rot_diff", "cos_diff", "sin_diff")
        todo = [(z[:, 2 * h:2 * h + 2, :], P2(g), r, t_d[n]) for z, g, r, n in
                ((B["dq"], "g_dq", B["rot_dq"], "q"), (B["dk"], "g_dk", B["rot_dk"], "k")) for h in range(2)]
        yield from rope_norms(todo, slice(0, 128), "blk64", names, 64, lambda n: 64 if n < 2 else 1, B)

    def stick_breaking(B, toks):
        sq_, sk, sv, sp, ex, spm, exm = (B[n] for n in ("sbq", "sbk", "sbv", "sp", "ex", "spm", "exm"))
        read = []
        diag = lambda z: z.rearrange("p s (a b c) -> p s a b c", a=2, b=2)[:, :, :, 0, :]

        def apply(p, done):
            prog.wait(PE, done, free[YB_])
            for s in range(2):
                v = slice(128 * p + 64 * s, 128 * p + 64 * s + 64)
                y = ps[64 * s:64 * s + 64, YB_, :]
                nc.tensor.matmul(y[:, :TOK2], sv[:META, 2, v], exm[:, s, :], start=True, stop=True, skip_group_check=True)
                nc.tensor.matmul(y[:, META:TOK2], sv[:, 0, v], ex[:, s, :SEQ], start=False, stop=True, skip_group_check=True)
                m = nc.tensor.matmul(y[:, META + 128:TOK2], sv[:, 1, v], ex[:, s, SEQ:], start=False, stop=True,
                                     skip_group_check=True)
            m = prog.mark(PE, m)
            free[YB_] = output(B, (ALL, p), ps[:, YB_, :TOK2], m)
            return m

        done = None
        for p in range(5):
            if p >= 1:
                while B["o_busy"]:
                    yield
                read = [apply(p - 1, done)]
            if p == 4:
                break
            prog.wait(PE, free[SB_], free[TB_], free[TB_ + 1], *toks)
            for s in range(2):
                rows = slice(64 * s, 64 * s + 64)
                q, k = sq_[rows, p, :], sk[rows, p, :]
                nc.tensor.matmul(ps[:, SB_ + s, :SEQ], k[:, META:META + 128], q[:, META:], start=True, stop=True, skip_group_check=True)
                nc.tensor.matmul(ps[:, SB_ + s, SEQ:384], k[:, META + 128:], q[:, META + 128:], start=False, stop=True,
                                 skip_group_check=True)
                m = nc.tensor.matmul(ps[:META, TB_ + s, :TOK2], k[:, :META], q, start=True, stop=True, skip_group_check=True)
            m = prog.mark(PE, m)
            z, zm = ps[:, SB_:SB_ + 2, :384], ps[:META, TB_:TB_ + 2, :TOK2]
            prepared = []
            for src, t, dst in ((z, ex[:, :, :], sp[:, :, :384]), (zm, exm[:, :, :], spm[:, :, :])):
                a = on(SC, m, *read)(nc.scalar.activation, t, src, ACT.Abs)
                a = on(SC, a)(nc.scalar.activation, t, t, ACT.Exp, scale=-1.0)
                a = on(SC, a)(nc.scalar.activation, t, t, ACT.Ln, bias=C("ones", slice(0, t.shape[0]))[:, 0:1])
                prepared.append(on(VE, a)(nc.vector.scalar_tensor_tensor, dst, src, 0.0, t, ALU.max, ALU.add))
            one = C("strict_01").unsqueeze(1).unsqueeze(1).to_broadcast([128, 2, 2, 128])
            a = on(VE, prepared[0])(nc.vector.tensor_tensor, diag(sp), diag(sp), one, ALU.mult)
            last = spm[:, :, :META]
            b = on(VE, prepared[1])(nc.vector.tensor_tensor, last, last, C("strict_01", slice(0, META))[:, :META]
                                    .unsqueeze(1).to_broadcast([META, 2, META]), ALU.mult)
            yield
            yield
            prog.wait(PE, a, b)

            def add(dst, lhs, rhs):
                return nc.tensor.matmul(dst, lhs, rhs, start=False, stop=True, skip_group_check=True)

            for s in range(2):
                zs, s0, s1 = ps[:, SB_ + s, :], sp[:, s, :SEQ], sp[:, s, SEQ:384]
                add(zs[:, :SEQ], C("suffix"), s0)
                add(zs[:, 128:SEQ], C("minus"), s1)
                add(zs[:, :128], ident_b[:, :], strict_b[:, :])
                add(zs[:, SEQ:384], C("suffix"), s1)
                m = add(zs[:, SEQ:384], ident_b[:, :], strict_b[:, :])
            m0 = prog.mark(PE, m)
            for s in range(2):
                zs, s0, s1 = ps[:META, TB_ + s, :], sp[:, s, :SEQ], sp[:, s, SEQ:384]
                add(zs[:, :TOK2], C("suffix")[:META, :META], spm[:, s, :])
                add(zs[:, META:TOK2], C("minus")[:, :META], s0)
                add(zs[:, META + 128:TOK2], C("minus")[:, :META], s1)
                m = add(zs[:, :META], ident_b[:META, :META], strict_b[:META, :META])
            m1 = prog.mark(PE, m)
            a = on(SC, m0)(nc.scalar.activation, ex[:, :, :], z, ACT.Exp)
            b = on(SC, m1)(nc.scalar.activation, exm[:, :, :], zm, ACT.Exp)
            free[SB_], free[TB_], free[TB_ + 1] = a, b, b
            done = [a, b]
            yield

    def differential(B, heads, t_v):
        dq, dk, dv, rn = B["dq"], B["dk"], B["dv"], B["rn"]
        ready = B["normed"] + t_v
        B["rn_read"] = B["normed"]

        def combine(E, f, a, m, L):
            a = on(VE, a)(nc.vector.tensor_tensor, f[:, 1:2], f[:, 1:2], B["neg_lam"][:m, :], ALU.mult)
            a = on(VE, a)(nc.vector.tensor_scalar, E[:, 1, :], E[:, 1, :], f[:, 1:2], None, ALU.mult)
            return on(VE, a)(nc.vector.scalar_tensor_tensor, E[:, 0, :], E[:, 0, :], f[:, 0:1], E[:, 1, :], ALU.mult, ALU.add)

        pending, sq_read = [], [None, None]

        def normalise():
            h, t = pending.pop(0)
            m = on(PE, t, free[TB_])(nc.tensor.matmul, ps[:, TB_, :TOK2], C("ones"), sq[:, h % 2, :TOK2], start=True, stop=True)
            sq_read[h % 2] = m
            r = inverse_rms(rn[:, 0, :], ps[:, TB_, :TOK2], 128, 1, m, *B["rn_read"])
            free[TB_] = r
            a = on(VE, r, t)(nc.vector.scalar_tensor_tensor, B["o"][:, h, :], B["o"][:, h, :], B["g_out"][:, :],
                             rn[:, 0, :], ALU.mult, ALU.mult)
            B["rn_read"] = [a]
            output(B, (ALL, h), B["o"][:, h, :], a)

        def meta_done(src, a):
            B["meta_copied"] = on(SC, a)(nc.scalar.activation, B["o"][:, :, :META], src, ACT.Copy)
            return B["meta_copied"]

        def finish(h, a):
            c = on(SC, a)(nc.scalar.activation, B["o"][:, h, META:], ps[:, YB_, META:TOK2], ACT.Copy)
            t = on(SC, c, B["meta_copied"], sq_read[h % 2])(nc.scalar.activation, sq[:, h % 2, :TOK2], B["o"][:, h, :], ACT.Square)
            pending.append((h, t))
            return t

        steps = softmax_attention(
            B, lambda g, s: dq[64 * s:64 * s + 64, g, :], lambda g, s: dk[64 * s:64 * s + 64, g, :],
            lambda g, s, kt: dv[:TILES[kt][1], kt, 128 * g:128 * g + 128], 1, combine, meta_done, finish, ready)
        for _ in steps:
            yield
            if pending and not B["o_busy"]:
                normalise()
        while pending:
            normalise()

    def second_layer(i):
        nt = TOK2
        stream.start_layer(i + DEPTH, COLS2)
        nc.scalar.dma_start(params[:, :n_par2], ins["params2"][bass.ds(i, 1)].rearrange("a p n -> (a p) n"))\
            .then_inc(loaded, 16)
        act = (h_hi, h_lo)
        norm["pending"] = (nt, TILES)

        with ExitStack() as own:
            def buf(name, *shape, dt=F32, into=own.enter_context, parts=128):
                return sbuf("b2_" + name, parts, *shape, dt=dt, into=into)

            merged, gate = buf("mq_or_merged", KC, nt), buf("gate", KC, nt)
            attn = ExitStack()

            def tmp_buf(name, *shape, dt=F32, into=attn.enter_context, parts=128):
                return buf(name, *shape, dt=dt, into=into, parts=parts)

            B = {"mv": tmp_buf("mv", 3, 512), "sbv": tmp_buf("sbv", 3, 512), "dv": tmp_buf("dv", 3, 512),
                 "sbq": tmp_buf("sbq", 4, nt), "sbk": tmp_buf("sbk", 4, nt), "dq": tmp_buf("dq", 4, nt),
                 "dk": tmp_buf("dk", 4, nt), "o": tmp_buf("o", 4, nt), "rn": tmp_buf("rn", 2, nt),
                 "rot": tmp_buf("rot", 2, nt), "kr": tmp_buf("kr", nt), "small": tmp_buf("small", 2, 3, 8),
                 "neg_lam": tmp_buf("neg_lam", 1), "g_out": tmp_buf("g_out", 1), "lam": tmp_buf("lam_sums", 2),
                 "mq": merged, "o_his": [], "o_lows": [], "o_read": [], "o_busy": False}
            o_hi, o_lo = (tmp_buf(f"o_{n}", 4, nt, dt=F32R) for n in ("hi", "lo"))
            B["o_hi"], B["o_lo"] = o_hi, o_lo
            for n in ("rot_q", "rot_dq", "rot_dk"):
                B[n] = tmp_buf(n, 128)
            shared = ExitStack()
            B["mk"] = buf("mk", 8, nt, into=shared.enter_context)
            inner = ExitStack()
            c32 = gate[:, 0:3, :]
            c_hi, c_lo = (buf(f"c_{n}", 3, nt, dt=F32R, into=inner.enter_context) for n in ("hi", "lo"))
            t_c, t_kr = [], []
            project(0, KC, act, nt, track(normed_to(lambda c: c32[:, c, :], nt), t_c))
            for e in (SC, VE, PE, PO):
                prog.engines[e].wait_ge(loaded, 16)
            lam = P2("lam").rearrange("p (a b) -> p a b", b=2)
            a = on(VE)(nc.vector.tensor_tensor, B["lam"][:, :], lam[:, :, 0], lam[:, :, 1], ALU.mult)
            m = on(PE, a, free[TB_ + 1])(nc.tensor.matmul, ps[:, TB_ + 1, 0:2], C("ones"), B["lam"][:, :], start=True, stop=True)
            a = on(SC, m)(nc.scalar.activation, B["lam"][:, :], ps[:, TB_ + 1, 0:2], ACT.Exp)
            free[TB_ + 1] = a
            a = on(VE, a)(nc.vector.tensor_tensor, B["neg_lam"][:, :], B["lam"][:, 1:2], B["lam"][:, 0:1], ALU.subtract)
            t_lam = on(VE, a)(nc.vector.tensor_tensor, B["neg_lam"][:, :], B["neg_lam"][:, :], P2("lam_init"), ALU.subtract)
            t_lam = on(VE, t_lam)(nc.vector.tensor_tensor, B["g_out"][:, :], P2("g_do"), P2("one_less"), ALU.mult)

            def latents(c, b, t):
                r, rows = rs_of(nt), slice(64, 96)
                if c == 0:
                    t_c.append(on(VE, t)(nc.vector.tensor_tensor, c32[:, 2, :], ps[:, b, :nt], r, ALU.mult))
                    return t_c[-1]
                t_kr.append(on(VE, t)(nc.vector.tensor_tensor, B["kr"][rows, :], ps[rows, b, :nt], r[rows, :], ALU.mult))
                return t_kr[-1]
            project(1, KC, act, nt, latents)
            t_latent = []

            def norm_latents():
                prev = None
                for first, n, gain in ((0, 2, "g_cq"), (2, 1, "g_ckv")):
                    sqs = [on(SC, *t_c, prev)(nc.scalar.activation, sq[:, k, :nt], c32[:, first + k, :], ACT.Square)
                           for k in range(n)]
                    yield
                    prog.wait(PE, free[TB_], *sqs)
                    for k in range(n):
                        m = nc.tensor.matmul(ps[:, TB_, :nt], C("ones"), sq[:, k, :nt], start=k == 0, stop=k == n - 1)
                    prev = m = prog.mark(PE, m)
                    rd = t_latent[-1] if t_latent else None
                    r = inverse_rms(B["rn"][:, 0, :], ps[:, TB_, :nt], 128 * n, 1, m, rd)
                    free[TB_] = r
                    for k in range(n):
                        v = c32[:, first + k, :]
                        a = on(VE, r)(nc.vector.scalar_tensor_tensor, v, v, P2(gain)[:, k:k + 1], B["rn"][:, 0, :], ALU.mult, ALU.mult)
                        t_latent.append(a)
                        split_done.append(split(v, c_hi[:, first + k, :], c_lo[:, first + k, :], a))
                    yield
            split_done = []
            state["filler"] = norm_latents()
            t_sb = []

            for n in range(2):
                project(2 + n, KC, act, nt, track(normed_to(lambda c, n=n: B["sbq"][:, 2 * n + c, :], nt, 0.125), t_sb))
            for n in range(2):
                project(4 + n, KC, act, nt, track(normed_to(lambda c, n=n: B["sbk"][:, 2 * n + c, :], nt), t_sb))
            finish_filler()
            heads = {"q": [], "k": [], "kr": t_kr}
            hs, ls = zip(*split_done)
            project(6, 2, (c_hi, c_lo), nt, track(copy_to(lambda c: B["mq"][:96, c, :]), heads["q"]), hs[:2], ls[:2])
            w = stream.view(7, 1)
            for t_ in range(8):
                b = next_bank()
                prog.wait(PE, free[b])
                cols = slice(128 * t_, 128 * t_ + 128)
                t = stream.product(7, ps[:, b, :nt], [((w[0][:, 0, cols], w[1][:, 0, cols]),
                                                       (c_hi[:, 2, :], c_lo[:, 2, :]), True)], his=[hs[2]], lows=[ls[2]])
                heads["k"].append(on(SC, t)(nc.scalar.activation, B["mk"][0:64, t_, :], ps[0:64, b, :nt], ACT.Copy))
                free[b] = heads["k"][-1]
            t_v = []
            w = [z.rearrange("p k (h two d) -> p k h two d", h=8, two=2)[:, 0, :, 1, :] for z in w]
            for n, (a0, m) in enumerate(TILES):
                b = next_bank()
                prog.wait(PE, free[b])
                lhs = [z[:, 2, a0:a0 + 128] for z in (c_hi, c_lo)]
                t = stream.product(7, ps[:, b, :], [(lhs, w, False)])
                later.append(stream.split_next(n)) if n < 2 else flush()
                t_v.append(on(SC, t)(nc.scalar.activation, B["mv"][:m, n, :], ps[:m, b, :], ACT.Copy))
                free[b] = t_v[-1]
            for n in (8, 9):
                stream.used[n] = prog.now(PE)[0]
                flush()
                stream.split_next(0)()
                stream.split_next(1)()
            inner.close()
            for e in (SC, VE, PE, PO):
                prog.engines[e].wait_ge(consts_in, 2 * 16)
            on(SC)(nc.scalar.activation, strict_b[:, :], C("strict_neg"), ACT.Copy)
            work = ExitStack()
            top = work.enter_context
            B["ksq"], B["rn_k"], B["rot_k"] = gate[:96, 0:2, :], gate[:96, 2:4, :], gate[:96, 4, :]
            B["e"] = B["o"][:, :, :].rearrange("p (a b) t -> p a b t", a=2)
            B["pt"], B["ptm"] = buf("pt", 512, into=top)[:, :], buf("ptm", 256, into=top, parts=META)[:, :]
            for e in (SC, VE, PO):
                prog.wait(e, prog.now(PE, SC, VE, PO))
            B["gains_done"] = [on(PO)(nc.gpsimd.tensor_scalar, B[dst][rows, :], C(rot, rows), P2(g, rows), None, ALU.mult)
                               for dst, rot, g, rows in (("rot_q", "rot_mla", "g_q", slice(0, 96)),
                                                         ("rot_dq", "rot_diff", "g_dq", slice(0, 128)),
                                                         ("rot_dk", "rot_diff", "g_dk", slice(0, 128)))]
            t_sv, t_d, t_dv = [], {"q": [], "k": []}, []
            state["filler"] = mla(B, heads, t_v, t_d)

            def values(u, dst, into):
                for n in range(2):
                    to = normed_tokens_to(lambda c, n=n: dst[:TILES[c][1], c, 256 * n:256 * n + 256], TILES)
                    project_tokens(u + n, KC, act, TILES, 256, track(to, into))

            values(10, B["sbv"], t_sv)
            for n in range(2):
                project(12 + n, KC, act, nt, track(normed_to(lambda c, n=n: B["dq"][:, 2 * n + c, :], nt), t_d["q"]))
            for n in range(2):
                project(14 + n, KC, act, nt, track(normed_to(lambda c, n=n: B["dk"][:, 2 * n + c, :], nt), t_d["k"]))
            values(16, B["dv"], t_dv)
            u, merged_done, branch_read = 18, [], []
            t_gate = []
            for branch in range(3):
                t_gate = []
                for n in range(4):
                    def evacuate(c, b, t, n=n):
                        return on(VE, t, *branch_read)(nc.vector.tensor_tensor, gate[:, 2 * n + c, :], ps[:, b, :nt],
                                                       rs_of(nt), ALU.mult)
                    project(u + n, KC, act, nt, track(evacuate, t_gate))
                u += 4
                finish_filler()
                flush()
                if branch == 0:
                    work.close()
                    shared.close()
                    B["ex"] = B["o"][:, :, :].rearrange("p k t -> p (k t)")[:, :768].rearrange("p (a b) -> p a b", a=2)
                    B["sp"] = B["mv"][:, 0:2, :]
                    B["exm"], B["spm"] = (tmp_buf(n, 2, nt, parts=META) for n in ("exm", "spm"))
                    B["e"], B["pt"] = tmp_buf("e2", 2, 2, nt)[:, :, :, :], B["mv"][:, 2, :]
                    B["ptm"] = tmp_buf("ptm2", 256, parts=META)[:, :]
                    for e in (SC, VE, PO):
                        prog.wait(e, prog.now(PE, SC, VE, PO))
                t_sig = []

                def sigmoids(until, branch=branch, t_gate=t_gate, t_sig=t_sig):
                    for k in range(len(t_sig), until):
                        t_sig.append(on(SC, t_gate[k])(nc.scalar.activation, gate[:, k, :], gate[:, k, :], ACT.Sigmoid,
                                                       bias=P2("gate_b")[:, KC * branch + k:KC * branch + k + 1]))
                sigmoids(2)
                o_hs, o_ls = B["o_his"], B["o_lows"]
                B["o_his"], B["o_lows"], B["o_busy"] = [], [], True
                if branch == 1:
                    prog.wait(VE, t_lam)
                following = (stick_breaking(B, t_sb + t_sv), differential(B, t_d, t_dv), None)[branch]

                def merge(n, branch=branch, t_sig=t_sig, following=following):
                    def evacuate(c, b, t):
                        k = 4 * n + c
                        if k < 3:
                            sigmoids(4 + 2 * k if k < 2 else KC)
                        if k == 2:
                            nc.scalar.preload_act_table_set("natural_log_exp_and_others")
                            state["filler"] = following
                        if branch == 0:
                            a = on(VE, t, t_sig[k])(nc.vector.tensor_tensor, merged[:, k, :], gate[:, k, :], ps[:, b, :nt], ALU.mult)
                            merged_done.append(a)
                            branch_read.append(a)
                            return a
                        a = on(VE, t, t_sig[k])(nc.vector.tensor_tensor, gate[:, k, :], gate[:, k, :], ps[:, b, :nt], ALU.mult)
                        c = on(PO, a, merged_done[k])(nc.gpsimd.tensor_tensor, merged[:, k, :], merged[:, k, :], gate[:, k, :], ALU.add)
                        merged_done[k] = c
                        branch_read.append(c)
                        return a
                    return evacuate

                branch_read.clear()
                for n in range(2):
                    project(u + n, 4, (o_hi, o_lo), nt, merge(n), o_hs, o_ls)
                u += 2
                B["o_read"], B["o_busy"] = prog.now(PE), False
            flush()
            attn.close()
            mix = [buf(f"mix_{n}", KC, nt, dt=F32R) for n in ("hi", "lo")]
            h_read = prog.now(PE)
            for e in (SC, VE, PO):
                prog.wait(e, prog.now(PE, VE))
            his, lows = [], []
            for k in range(KC):
                th, tl = split(merged[:, k, :], mix[0][:, k, :], mix[1][:, k, :], merged_done[k], low_on=VE if k % 2 else PO)
                his.append(th)
                lows.append(tl)
            x_done, next_his, next_lows = [], [], []
            for n in range(4):
                project(u + n, KC, mix, nt, add_to_residual(nt, 2 * n, x_done, P2("g_ln2"), act, next_his, next_lows,
                                                            *h_read), his, lows)
            u += 4
        norm["pending"] = (nt,)
        u = mlp(u, nt, next_his, next_lows, "b2", P2("g_next"), act, [], [])
        assert u == UNITS
        flush()

    rounds = [PE, SC, VE, PO]
    kinds = [prog.engines[e].engine for e in rounds]
    counts = [prog.sems[e] for e in rounds] + [loaded]
    numbers = range(counts[0].num, counts[-1].num + 1)

    def next_round():
        nc.multi_engine_barrier(kinds, sems_to_clear=numbers)
        prog.restart()
        for b in free:
            free[b] = None
        restart_norms()

    def first_constants():
        nc.sync.dma_start(consts[:, own0:own0 + n1], ins["consts"][:, own0:own0 + n1]).then_inc(consts_in, 16)

    nc.sync.dma_start(x[:, :, META:], ins["x"]).then_inc(loaded, 16)
    stream.load_all(ins["stream"], first_constants)
    nc.scalar.dma_start(start_gains[:, :], ins["start_gains"]).then_inc(loaded, 16)
    nc.scalar.dma_start(x[:, :, :META], ins["meta"]).then_inc(loaded, 16)
    nc.scalar.dma_start(consts[:, :own0], ins["consts"][:, :own0]).then_inc(both_in, 16)
    nc.scalar.preload_act_table_set("natural_log_exp_and_others")
    for e in rounds:
        prog.engines[e].wait_ge(loaded, 3 * 16)
    restart_norms()
    for k in range(KC):
        prepare(k, SEQ, start_gains[:, :KC], (h_hi, h_lo), None, [], [], at_start=True)
        flush()
    stream.split_first()
    xm = x[:, :, :META]
    packed = lambda z: z[:, 0, :KC * META].rearrange("p (k t) -> p k t", k=KC)
    a = on(VE)(nc.vector.tensor_tensor, packed(tmp), xm,
               start_gains[:, KC:].unsqueeze(2).to_broadcast([128, KC, META]), ALU.mult)
    split(packed(tmp), h_hi[:, :, :META], h_lo[:, :, :META], a)
    a = on(SC, norm["summed"])(nc.scalar.activation, packed(sq), xm, ACT.Square)
    on(VE, a)(nc.vector.reduce_sum, sums[:, :META], packed(sq).rearrange("p k t -> p t k"), AX)
    for e in rounds:
        prog.engines[e].wait_ge(both_in, 16)
    for dst, name in ((ident_b, "ident"), (causal_b, "causal_neg")):
        on(SC)(nc.scalar.activation, dst[:, :], C(name), ACT.Copy)
    next_round()
    with nc.Fori(0, DEPTH, engines=kinds) as i:
        first_layer(i)
        next_round()
    if LAYERS > DEPTH:
        nc.scalar.dma_start(consts[:, own0:own0 + n2], ins["consts"][:, own0 + n1:]).then_inc(consts_in, 16)
        with nc.Fori(0, DEPTH, engines=kinds) as i:
            second_layer(i)
            next_round()
    nc.scalar.dma_start(out, x[:, :, META:]).then_inc(stored, 16)
    nc.scalar.wait_ge(stored, 16)


def _chunks(w, kcs):
    n = w.shape[1]
    u = np.ascontiguousarray(w.reshape(kcs, 128, n).transpose(1, 0, 2)).reshape(128, kcs * n)
    return np.pad(u, ((0, 0), (0, UNIT - u.shape[1]))) if u.shape[1] < UNIT else u


def _units(w, kcs, cols):
    return [_chunks(w[:, a:a + cols], kcs) for a in range(0, w.shape[1], cols)]


def _first_units(a, i):
    w = a["w_in"][i]
    at = np.cumsum([0, 512, 128, 128, 128, 128, 128, 128, 24, 512, 512, 512, 512, 1024, 1024])
    q, kc, vc, ks, vs, kw, vw, gate, rq, rk, rv, rg, ma, mb = (w[:, at[n]:at[n + 1]] for n in range(14))
    twice = lambda z: z.reshape(D, 2, 1, 64).repeat(2, axis=2).reshape(D, 256)
    heads = lambda z: z.reshape(-1, 2, 4, 64).transpose(0, 2, 1, 3).reshape(-1, 512)
    w1 = [_chunks(a[n][i][r:r + D], KC) for n in ("cmp_w1_k", "cmp_w1_v") for r in (0, D)]
    units = [_chunks(twice(kc), KC), _chunks(twice(vc), KC)]
    others = _units(heads(q), KC, 256) + [_chunks(np.concatenate([ks, kw], 1), KC), _chunks(np.concatenate([vs, vw], 1), KC)]
    for pair in zip(others, w1):
        units += pair
    units.append(_chunks(gate, KC))
    for z in (rq, rk, rv, rg, ma, mb):
        units += _units(z, KC, 256)
    up = a["w_up_nsa"][i].reshape(2, 4, 64, D).transpose(1, 0, 2, 3).reshape(512, D)
    units += _units(up, 4, 512) + _units(a["w_up_ret"][i], 4, 512) + _units(a["w_out"][i], KC, 256)
    units += _units(a["w_ff1"][i], KC, 256)
    for c in range(0, D, 256):
        units += [_chunks(a["w_ff2"][i][r:r + D, c:c + 256], KC) for r in range(0, FF, D)]
    units += _units(a["w_ple"][i], 2, D) + _units(a["w_ple_gate"][i], KC, 256)
    return units


def _columns(v):
    return v.reshape(-1, 128).T


def _first_params(a, i):
    twice = lambda v: np.concatenate([v, v])[:, None]
    rows = lambda z: z.reshape(16, 2, 64).transpose(1, 2, 0).reshape(128, 16)
    w2 = lambda z: z.reshape(2, 128, 64).transpose(1, 0, 2).reshape(128, 128)
    p = a["p"][i, 0].T.reshape(2, 128, SEQ).transpose(1, 0, 2).reshape(128, 2 * SEQ)
    following = a["norm_mix"][i + 1] if i + 1 < DEPTH else a["ln1_g_2"][0]
    return np.concatenate([_columns(a["norm_mlp"][i]), _columns(a["norm_ple"][i]), _columns(following),
                           twice(a["nsa_q_norm"][i]), twice(a["nsa_k_norm"][i]), rows(a["cmp_pos_k"][i]),
                           rows(a["cmp_pos_v"][i]), w2(a["cmp_w2_k"][i]), w2(a["cmp_w2_v"][i]), p], axis=1)


def _second_units(a, i):
    w = a["w_in_2"][i]
    at = np.cumsum([0, 256, 128, 32, 512, 512, 512, 512, 512, 512, 3 * D])
    cq, ckv, kr, sq, sk, sv, dq, dk, dv, gates = (w[:, at[n]:at[n + 1]] for n in range(10))
    units = [_chunks(cq, KC), _chunks(np.concatenate([ckv, np.pad(kr, ((0, 0), (64, 32)))], 1), KC)]
    for z in (sq, sk):
        units += _units(z, KC, 256)
    uq = np.pad(a["mla_w_uq_2"][i].reshape(256, 8, 96), ((0, 0), (0, 0), (0, 32))).reshape(256, 1024)
    units += [_chunks(uq, 2), _chunks(a["mla_w_ukv_2"][i], 1)]
    units += [np.zeros((128, UNIT), np.float32)] * 2
    for z in (sv, dq, dk, dv):
        units += _units(z, KC, 256)
    for n in range(3):
        units += _units(gates[:, n * D:n * D + D], KC, 256)
        units += _units(a["w_branch_2"][i][512 * n:512 * n + 512], 4, 512)
    units += _units(a["w_out_2"][i], KC, 256) + _units(a["w_ff1_2"][i], KC, 256)
    for c in range(0, D, 256):
        units += [_chunks(a["w_ff2_2"][i][r:r + D, c:c + 256], KC) for r in range(0, FF, D)]
    return units


def _second_params(a, i):
    def rows(v, *at):
        out = np.zeros((128, 1), np.float32)
        for b in at:
            out[b:b + len(v), 0] = v
        return out

    lam = np.zeros((128, 4), np.float32)
    lam[:64] = a["diff_lambda_2"][i].T
    lam_init = 0.8 - 0.6 * np.exp(-0.3 * i)
    full = lambda v: np.full((128, 1), v, np.float32)
    following = a["ln1_g_2"][min(i + 1, DEPTH - 1)]
    return np.concatenate([_columns(a["ln2_g_2"][i]), _columns(following), _columns(a["mla_cq_norm_g_2"][i]),
                           _columns(a["mla_ckv_norm_g_2"][i]), rows(a["mla_q_norm_g_2"][i], 0),
                           rows(a["mla_k_norm_g_2"][i], 0), rows(a["diff_q_norm_g_2"][i], 0, 64),
                           rows(a["diff_k_norm_g_2"][i], 0, 64), _columns(a["diff_out_norm_g_2"][i]), lam,
                           full(lam_init), full(1.0 - lam_init), _columns(a["gate_b_2"][i])], axis=1)


def host_arrays(inputs):
    a = {k: np.asarray(v) for k, v in inputs.items()}
    units = []
    for i in range(DEPTH):
        units += _first_units(a, i)
    if LAYERS > DEPTH:
        for i in range(DEPTH):
            units += _second_units(a, i)
    arrays = {"stream": np.stack(units), "consts": np.concatenate(list(const_tables().values()), axis=1),
              "x": a["x"][0].T.reshape(KC, 128, SEQ).transpose(1, 0, 2),
              "meta": a["meta_tokens_2"].T.reshape(KC, 128, META).transpose(1, 0, 2),
              "start_gains": np.concatenate([_columns(a["norm_mix"][0]), _columns(a["ln1_g_2"][0])], axis=1),
              "params1": np.stack([_first_params(a, i) for i in range(DEPTH)])}
    if LAYERS > DEPTH:
        arrays["params2"] = np.stack([_second_params(a, i) for i in range(DEPTH)])
    assert arrays["stream"].shape == (LAYERS * UNITS, 128, UNIT)
    return {k: np.ascontiguousarray(v) for k, v in arrays.items()}


def kernel(**inputs):
    import concourse.bacc as bacc
    from concourse.bass_utils import run_bass_kernel_spmd

    nc = bacc.Bacc("TRN2", target_bir_lowering=False, num_devices=1)
    arrays, aps = {}, {}
    for name, v in host_arrays(inputs).items():
        arrays[f"in_{name}"] = v
        aps[name] = nc.dram_tensor(f"in_{name}", v.shape, mybir.dt.from_np(v.dtype), kind="ExternalInput").ap()
    out = nc.dram_tensor("out_x", (128, KC, SEQ), F32, kind="ExternalOutput").ap()
    build(nc, aps, out)
    r = run_bass_kernel_spmd(nc, [arrays], core_ids=[0])
    y = np.asarray(r.results[0]["out_x"]).reshape(128, KC, SEQ)
    return np.ascontiguousarray(y.transpose(2, 1, 0)).reshape(1, SEQ, D)
```
